# Optimizing a Trainium2 kernel written in Bass

```python
import math
import jax, jax.numpy as jnp
from jax import lax
import numpy as np

D_MODEL = 1024
BATCH = 1
SEQ = 1024
DEPTH = 2

CHUNK = 64
HEAD_DIM = 64
A_HEADS = 4
A_WIDTH = A_HEADS * 2 * HEAD_DIM
B_HEADS = 8
B_KV_HEADS = 2
B_GROUP = B_HEADS // B_KV_HEADS
B_PREV_CHUNKS = 1
B_WIDTH = B_HEADS * HEAD_DIM
B_KV_WIDTH = B_KV_HEADS * HEAD_DIM
C_HEADS = 16
C_PREV_CHUNKS = 8
C_BAND = (C_PREV_CHUNKS + 1) * CHUNK
C_WIDTH = C_HEADS * HEAD_DIM
REL_CLIP = 256
Q_BLOCK = 128
AB_SIZES = (A_WIDTH, A_WIDTH, A_WIDTH, B_WIDTH, B_KV_WIDTH, B_KV_WIDTH, A_WIDTH, B_WIDTH)
AB_IN = sum(AB_SIZES)
AB_SPLITS = tuple(int(s) for s in np.cumsum(AB_SIZES)[:-1])
C_IN = 4 * C_WIDTH
N_AB = (DEPTH + 1) // 2
N_C = DEPTH // 2
EPS = 1e-6
NEG = -1e30

kernel_name = 'hybrid_diff_swa_chunkrel_encoder'

def rms_norm(x, g):
    x32 = x.astype(jnp.float32)
    y = x32 * lax.rsqrt(jnp.mean(x32 * x32, axis=-1, keepdims=True) + EPS)
    return (y * g.astype(jnp.float32)).astype(x.dtype)

def alibi_slopes(n):
    return 2.0 ** (-8.0 * jnp.arange(1, n + 1, dtype=jnp.float32) / n)

def chunk_band(t, n_prev):
    nc = t.shape[1]
    pad = [(0, 0)] * t.ndim
    pad[1] = (n_prev, 0)
    tp = jnp.pad(t, pad)
    return jnp.concatenate([tp[:, j:j + nc] for j in range(n_prev + 1)], axis=2)

def diff_attention(q, k, v, lq1, lk1, lq2, lk2, subln_g, lam_init):
    bsz, slen = q.shape[0], q.shape[1]
    nqb = slen // Q_BLOCK
    scale = HEAD_DIM ** -0.5
    lam = (jnp.exp(jnp.sum(lq1.astype(jnp.float32) * lk1.astype(jnp.float32)))
           - jnp.exp(jnp.sum(lq2.astype(jnp.float32) * lk2.astype(jnp.float32))) + lam_init)
    slopes = alibi_slopes(A_HEADS)
    key_pos = jnp.arange(slen)
    q_blocks = q.reshape(bsz, nqb, Q_BLOCK, A_HEADS, 2, HEAD_DIM).swapaxes(0, 1)

    def one_block(args):
        qb, i = args
        qpos = i * Q_BLOCK + jnp.arange(Q_BLOCK)
        s = jnp.einsum('bqhcd,bkhcd->bhcqk', qb, k).astype(jnp.float32) * scale
        dist = jnp.abs(qpos[:, None] - key_pos[None, :]).astype(jnp.float32)
        allowed = (key_pos[None, :] // CHUNK) <= (qpos[:, None] // CHUNK)
        s = s - slopes[None, :, None, None, None] * dist
        s = jnp.where(allowed, s, NEG)
        p = jax.nn.softmax(s, axis=-1)
        a = p[:, :, 0] - lam * p[:, :, 1]
        return jnp.einsum('bhqk,bkhe->bqhe', a.astype(v.dtype), v)

    o = lax.map(one_block, (q_blocks, jnp.arange(nqb)))
    o = o.swapaxes(0, 1).reshape(bsz, slen, A_HEADS, 2 * HEAD_DIM)
    o = rms_norm(o, subln_g) * (1.0 - lam_init)
    return o.reshape(bsz, slen, A_WIDTH)

def sliding_window_gqa(q, k, v, sinks):
    bsz, slen = q.shape[0], q.shape[1]
    nc = slen // CHUNK
    band = (B_PREV_CHUNKS + 1) * CHUNK
    scale = HEAD_DIM ** -0.5
    qc = q.reshape(bsz, nc, CHUNK, B_KV_HEADS, B_GROUP, HEAD_DIM)
    kb = chunk_band(k.reshape(bsz, nc, CHUNK, B_KV_HEADS, HEAD_DIM), B_PREV_CHUNKS)
    vb = chunk_band(v.reshape(bsz, nc, CHUNK, B_KV_HEADS, HEAD_DIM), B_PREV_CHUNKS)
    s = jnp.einsum('bcqkgd,bcskd->bckgqs', qc, kb).astype(jnp.float32) * scale
    i = jnp.arange(CHUNK)
    j = jnp.arange(band)
    dist = jnp.abs(B_PREV_CHUNKS * CHUNK + i[:, None] - j[None, :]).astype(jnp.float32)
    slopes = alibi_slopes(B_HEADS).reshape(B_KV_HEADS, B_GROUP)
    s = s - slopes[:, :, None, None] * dist
    key_abs = jnp.arange(nc)[:, None] * CHUNK - B_PREV_CHUNKS * CHUNK + j[None, :]
    s = jnp.where((key_abs >= 0)[None, :, None, None, None, :], s, NEG)
    sink = jnp.broadcast_to(sinks.astype(jnp.float32).reshape(1, 1, B_KV_HEADS, B_GROUP, 1, 1),
                            s.shape[:-1] + (1,))
    p = jax.nn.softmax(jnp.concatenate([s, sink], axis=-1), axis=-1)[..., :-1]
    o = jnp.einsum('bckgqs,bcskd->bcqkgd', p.astype(v.dtype), vb)
    return o.reshape(bsz, slen, B_WIDTH)

def chunked_relpos_attention(q, k, v, rel_table):
    bsz, slen = q.shape[0], q.shape[1]
    nc = slen // CHUNK
    pad = C_PREV_CHUNKS * CHUNK
    scale = HEAD_DIM ** -0.5
    kp = jnp.pad(k, ((0, 0), (pad, 0), (0, 0), (0, 0)))
    vp = jnp.pad(v, ((0, 0), (pad, 0), (0, 0), (0, 0)))
    i = jnp.arange(CHUNK)
    j = jnp.arange(C_BAND)
    rel = pad + i[:, None] - j[None, :]
    idx = jnp.clip(rel, -REL_CLIP, REL_CLIP) + REL_CLIP
    bias = rel_table[:, idx].astype(jnp.float32)
    qc = q.reshape(bsz, nc, CHUNK, C_HEADS, HEAD_DIM).swapaxes(0, 1)

    def one_chunk(args):
        qb, c = args
        kb = lax.dynamic_slice_in_dim(kp, c * CHUNK, C_BAND, axis=1)
        vb = lax.dynamic_slice_in_dim(vp, c * CHUNK, C_BAND, axis=1)
        s = jnp.einsum('bqhd,bkhd->bhqk', qb, kb).astype(jnp.float32) * scale + bias
        valid = (c * CHUNK - pad + j) >= 0
        s = jnp.where(valid, s, NEG)
        p = jax.nn.softmax(s, axis=-1)
        return jnp.einsum('bhqk,bkhd->bqhd', p.astype(vb.dtype), vb)

    o = lax.map(one_chunk, (qc, jnp.arange(nc)))
    return o.swapaxes(0, 1).reshape(bsz, slen, C_WIDTH)

def setup_inputs(seed: int = 0) -> dict:
    key = jax.random.key(seed)
    ks = jax.random.split(key, 16)
    f32 = jnp.float32
    x = jax.random.normal(ks[0], (BATCH, SEQ, D_MODEL), f32)
    pre_norm_g = 1.0 + 0.05 * jax.random.normal(ks[1], (DEPTH, D_MODEL), f32)
    post_norm_g = 1.0 + 0.05 * jax.random.normal(ks[2], (DEPTH, D_MODEL), f32)
    w_in_ab = jax.random.normal(ks[3], (N_AB, D_MODEL, AB_IN), f32) * D_MODEL ** -0.5
    w_out_ab = jax.random.normal(ks[4], (N_AB, A_WIDTH + B_WIDTH, D_MODEL), f32) * (A_WIDTH + B_WIDTH) ** -0.5
    diff_lambda_q1 = 0.1 * jax.random.normal(ks[5], (N_AB, HEAD_DIM), f32)
    diff_lambda_k1 = 0.1 * jax.random.normal(ks[6], (N_AB, HEAD_DIM), f32)
    diff_lambda_q2 = 0.1 * jax.random.normal(ks[7], (N_AB, HEAD_DIM), f32)
    diff_lambda_k2 = 0.1 * jax.random.normal(ks[8], (N_AB, HEAD_DIM), f32)
    diff_subln_g = 1.0 + 0.05 * jax.random.normal(ks[9], (N_AB, 2 * HEAD_DIM), f32)
    swa_sinks = 0.5 * jax.random.normal(ks[10], (N_AB, B_HEADS), f32)
    w_in_c = jax.random.normal(ks[11], (N_C, D_MODEL, C_IN), f32) * D_MODEL ** -0.5
    w_out_c = jax.random.normal(ks[12], (N_C, C_WIDTH, D_MODEL), f32) * C_WIDTH ** -0.5
    rel_bias = 0.2 * jax.random.normal(ks[13], (N_C, C_HEADS, 2 * REL_CLIP + 1), f32)
    return {'x': x, 'pre_norm_g': pre_norm_g, 'post_norm_g': post_norm_g,
            'w_in_ab': w_in_ab, 'w_out_ab': w_out_ab,
            'diff_lambda_q1': diff_lambda_q1, 'diff_lambda_k1': diff_lambda_k1,
            'diff_lambda_q2': diff_lambda_q2, 'diff_lambda_k2': diff_lambda_k2,
            'diff_subln_g': diff_subln_g, 'swa_sinks': swa_sinks,
            'w_in_c': w_in_c, 'w_out_c': w_out_c, 'rel_bias': rel_bias}

def reference(x, pre_norm_g, post_norm_g, w_in_ab, w_out_ab, diff_lambda_q1, diff_lambda_k1,
              diff_lambda_q2, diff_lambda_k2, diff_subln_g, swa_sinks, w_in_c, w_out_c, rel_bias):
    bsz, slen = x.shape[0], x.shape[1]
    for l in range(DEPTH):
        h = rms_norm(x, pre_norm_g[l])
        if l % 2 == 0:
            i = l // 2
            proj = jnp.einsum('bsd,de->bse', h, w_in_ab[i])
            qa, ka, va, qb, kb, vb, ga, gb = jnp.split(proj, AB_SPLITS, axis=-1)
            lam_init = 0.8 - 0.6 * math.exp(-0.3 * l)
            ya = diff_attention(qa.reshape(bsz, slen, A_HEADS, 2, HEAD_DIM),
                                ka.reshape(bsz, slen, A_HEADS, 2, HEAD_DIM),
                                va.reshape(bsz, slen, A_HEADS, 2 * HEAD_DIM),
                                diff_lambda_q1[i], diff_lambda_k1[i], diff_lambda_q2[i], diff_lambda_k2[i],
                                diff_subln_g[i], lam_init)
            yb = sliding_window_gqa(qb.reshape(bsz, slen, B_HEADS, HEAD_DIM),
                                    kb.reshape(bsz, slen, B_KV_HEADS, HEAD_DIM),
                                    vb.reshape(bsz, slen, B_KV_HEADS, HEAD_DIM),
                                    swa_sinks[i])
            y = jnp.concatenate([ya * jax.nn.silu(ga), yb * jax.nn.silu(gb)], axis=-1)
            y = jnp.einsum('bse,ed->bsd', y, w_out_ab[i])
        else:
            i = l // 2
            proj = jnp.einsum('bsd,de->bse', h, w_in_c[i])
            qc, kc, vc, gc = jnp.split(proj, 4, axis=-1)
            yc = chunked_relpos_attention(qc.reshape(bsz, slen, C_HEADS, HEAD_DIM),
                                          kc.reshape(bsz, slen, C_HEADS, HEAD_DIM),
                                          vc.reshape(bsz, slen, C_HEADS, HEAD_DIM),
                                          rel_bias[i])
            y = jnp.einsum('bse,ed->bsd', yc * jax.nn.silu(gc), w_out_c[i])
        x = x + rms_norm(y, post_norm_g[l])
    return x


_drawn_inputs = setup_inputs


def setup_inputs(seed=0):
    import zlib

    import numpy as np

    out = dict(_drawn_inputs(seed))
    spreads = {}
    factors = {'diff_lambda_q1': 8.0, 'swa_sinks': 2.854}
    for name, (base, spread) in spreads.items():
        noise = np.random.default_rng([zlib.crc32(name.encode()), seed]).standard_normal(out[name].shape)
        drawn = base * np.exp(spread * noise) if base else spread * noise
        out[name] = __import__('jax').numpy.asarray(drawn.astype(out[name].dtype))
    for name, factor in factors.items():
        out[name] = (out[name] * factor).astype(out[name].dtype)
    return out
```

```python
import math
from contextlib import ExitStack

import concourse.bass as bass
from concourse import mybir
from concourse.alu_op_type import AluOpType as ALU

F32 = mybir.dt.float32
F32R = mybir.dt.float32r
ACT = mybir.ActivationFunctionType

P = 128
SEQ = 1024
D = 1024
ST = SEQ // P
DT = D // P
HALF = 512
HD = 64
CHUNK = 64
A_HEADS, B_HEADS, C_HEADS = 4, 8, 16
REL_CLIP = 256
C_BAND_COLS = 5 * P
REL_ROW = 768
EPS = 1e-6
NEG = -1e30
HUGE = 3e38
LAM_INIT = 0.8 - 0.6 * math.exp(-0.3 * 0)
SCALE = HD ** -0.5


class Kind:

    def __init__(self, name, units, cols, out_row, first, per_unit, last_units):
        self.name = name
        self.units = units
        self.cols = cols
        self.out_row = out_row
        self.first = first
        self.per_unit = per_unit
        self.ahead = last_units
        self.steps = 16
        self.groups = 8 if name == "A" else 16
        self.pvs = self.groups // 2

    def tiles(self, t):
        first = {"A": 0, "B": max(0, t - 1), "C": max(0, t - 4)}[self.name]
        return first, t + 1 - first

    def step(self, j):
        return (j % 2, j // 2) if self.name == "A" else (j // 8, j % 8)

    def group_of_step(self, j):
        if self.name == "A":
            return j // 2 if j % 2 else None
        return j

    def group(self, g):
        return (0, g) if self.name == "A" else (g // 8, g % 8)


KIND_A = Kind("A", A_HEADS, dict(q=0, k=512, v=1024, g=2304), 0, ["v", "q", "k"], ["v"], ["q", "k"])
KIND_B = Kind("B", B_HEADS // 2, dict(q=1536, k=2048, v=2176, g=2816), 512, ["v", "k", "q"], [], ["q"])
KIND_C = Kind("C", C_HEADS // 2, dict(q=0, k=1024, v=2048, g=3072), 0, ["v", "q", "k"], ["v"], ["q", "k"])

STAGE_SLOT = dict(o=0, q=0, g=1, v=1, k=1)
PART_SLOT = dict(o=0, q=0, g=1, k=1, v=2)
FILLS = dict(o=16, g=2, v=2, q=2, k=2)
MMS = 48


def region1(kind, u, first, last):
    blocks = [("g", u)]
    if not first:
        blocks.append(("o", u - 1))
    if not last:
        blocks += [(b, u + 1) for b in kind.per_unit]
    return blocks


def region2(kind, u, last):
    return [] if last else [(b, u + 1) for b in kind.ahead]


def blocks_before(kind, u, first):
    if first:
        return [(b, 0) for b in kind.first]
    return region1(kind, u - 1, False, False) + region2(kind, u - 1, False)


def previous_on(slot_map, before, blocks, n):
    for b, v in reversed(before + blocks[:n]):
        if slot_map[b] == slot_map[blocks[n][0]]:
            return b, v
    return None


def fills_of(blocks):
    return [(b, v, f) for b, v in blocks for f in range(FILLS[b])]


def fill_ends(blocks):
    at, out = 0, []
    for b, v in blocks:
        for f in range(FILLS[b]):
            at += MMS // FILLS[b]
            out.append((at, b, v, f))
    return out


TAIL = 3


def slice_of(kind, u, first, last, s):
    n1 = MMS * len(region1(kind, u, first, last))
    n2 = MMS * len(region2(kind, u, last))
    if s < kind.steps:
        return n1 * s // kind.steps, n1 * (s + 1) // kind.steps
    t = s - kind.steps
    return n1 + n2 * t // TAIL, n1 + n2 * (t + 1) // TAIL


def done_fills(kind, u, first, last, s):
    lo, hi = slice_of(kind, u, first, last, s)
    blocks = region1(kind, u, first, last) + region2(kind, u, last)
    return [(b, v, f) for at, b, v, f in fill_ends(blocks) if lo < at <= hi]


def ge(eng, sem, value):
    if isinstance(value, int) and value <= 0:
        return
    eng.wait_ge(sem, value)


def ge_apart(eng, passed, *waits):
    for sem, value in waits:
        ge(eng, sem, value)
    if not all(isinstance(value, int) for _, value in waits):
        eng.sem_inc(passed, 1)


def phase_semaphore(nc, env, name):
    s = nc.alloc_semaphore(name)
    env["phase_semaphores"].append(s)
    return s


def retire(nc, env):
    nc.clear_and_free_semaphores(env["phase_semaphores"])
    env["phase_semaphores"] = []
    nc.all_engine_barrier()


def norm_phase(nc, layer, env, x_src, x_dst, post_g, pre_g):
    y, hT_hi, hT_lo, ident = env["y"], env["hT_hi"], env["hT_lo"], env["ident"]
    with ExitStack() as ctx:
        def sb(name, shape, dt=F32):
            return ctx.enter_context(nc.sbuf_tensor(f"n{layer}_{name}", shape, dt))

        def sem(name):
            return phase_semaphore(nc, env, f"n{layer}_{name}")

        xb = sb("xb", [P, 3, D])
        xn = sb("xn", [P, 3, D])
        scaled = sb("scaled", [P, 2, D])
        junk = sb("junk", [P, D])
        g_post = sb("g_post", [P, D])
        g_pre = sb("g_pre", [P, D])
        stat = sb("stat", [P, 6, ST])
        eps = sb("eps", [P, 1])
        tp = ctx.enter_context(nc.psum_tensor(f"n{layer}_tp", [P, 2, D], F32))
        x_loaded = [sem(f"x_loaded{i}") for i in range(3)]
        g_loaded, x_stored = sem("g_loaded"), [sem(f"x_stored{i}") for i in range(3)]
        consts, ysq, yroot, yrec, yscaled, xsum = (sem(n) for n in
                                                   ("consts", "ysq", "yroot", "yrec", "yscaled", "xsum"))
        xsq, xroot, xrec, xscaled, turned, hi_done, lo_done = (sem(n) for n in
                                                               ("xsq", "xroot", "xrec", "xscaled", "turned", "hi_done",
                                                                "lo_done"))
        post, pre = post_g is not None, pre_g is not None
        block = ctx.enter_context(nc.Block())
        lag = 2

        def x_tile(i):
            return xn[:, i % 3, :] if post else xb[:, i % 3, :]

        @block.sync
        def _(sp):
            if post:
                sp.dma_start(g_post[:], post_g.partition_broadcast(P)).then_inc(g_loaded, 16)
            if pre:
                sp.dma_start(g_pre[:], pre_g.partition_broadcast(P)).then_inc(g_loaded, 16)
            for i in range(ST + 1):
                if i < ST:
                    if i >= 3:
                        sp.wait_ge(xsum if post else xscaled, i - 2)
                        if not post:
                            sp.wait_ge(xsq, i - 2)
                    sp.dma_start(xb[:, i % 3, :], x_src[i * P:(i + 1) * P, :]).then_inc(x_loaded[i % 3], 16)
                if post and i >= 1:
                    sp.wait_ge(xsum, i)
                    sp.dma_start(x_dst[(i - 1) * P:i * P, :], xn[:, (i - 1) % 3, :]).then_inc(x_stored[(i - 1) % 3], 16)
            if post:
                for r in range(3):
                    sp.wait_ge(x_stored[r], 16 * ((ST - 1 - r) // 3 + 1))

        @block.gpsimd
        def _(pool):
            nc.gpsimd.memset(eps[:], EPS).then_inc(consts, 1)

        @block.scalar
        def _(act):
            act.wait_ge(consts, 1)
            for i in range(ST + lag):
                if post and i < ST:
                    nc.scalar.activation(junk[:], y[:, i, :], ACT.Square, accum_out=stat[:, 0, i:i + 1]).then_inc(ysq, 1)
                    act.wait_ge(ysq, i + 1)
                    nc.scalar.activation(stat[:, 1, i:i + 1], stat[:, 0, i:i + 1], ACT.Sqrt, scale=1.0 / D,
                                         bias=eps[:]).then_inc(yroot, 1)
                j = i - 1
                if pre and 0 <= j < ST:
                    if post:
                        act.wait_ge(xsum, j + 1)
                    else:
                        act.wait_ge(x_loaded[j % 3], 16 * (j // 3 + 1))
                    nc.scalar.activation(junk[:], x_tile(j), ACT.Square, accum_out=stat[:, 3, j:j + 1]).then_inc(xsq, 1)
                    act.wait_ge(xsq, j + 1)
                    nc.scalar.activation(stat[:, 4, j:j + 1], stat[:, 3, j:j + 1], ACT.Sqrt, scale=1.0 / D,
                                         bias=eps[:]).then_inc(xroot, 1)
                j = i - lag
                if pre and 0 <= j < ST:
                    act.wait_ge(turned, j + 1)
                    nc.scalar.activation(hT_hi[:, :, j * P:(j + 1) * P],
                                         tp[:, j % 2, :].rearrange("p (d s) -> p d s", d=DT), ACT.Copy).then_inc(hi_done, 1)

        @block.vector
        def _(dve):
            dve.wait_ge(g_loaded, 16 * (post + pre))
            for i in range(ST + lag):
                if post and i < ST:
                    dve.wait_ge(yroot, i + 1)
                    nc.vector.reciprocal(stat[:, 2, i:i + 1], stat[:, 1, i:i + 1]).then_inc(yrec, 1)
                    dve.wait_ge(yrec, i + 1)
                    if i >= 3:
                        dve.wait_ge(x_stored[i % 3], 16 * (i // 3))
                        if pre:
                            dve.wait_ge(xsq, i - 2)
                    nc.vector.scalar_tensor_tensor(out=xn[:, i % 3, :], in0=y[:, i, :], scalar=stat[:, 2, i:i + 1],
                                                   in1=g_post[:], op0=ALU.mult, op1=ALU.mult).then_inc(yscaled, 1)
                    dve.wait_ge(yscaled, i + 1)
                    dve.wait_ge(x_loaded[i % 3], 16 * (i // 3 + 1))
                    nc.vector.tensor_tensor(xn[:, i % 3, :], xn[:, i % 3, :], xb[:, i % 3, :], ALU.add).then_inc(xsum, 1)
                j = i - 1
                if pre and 0 <= j < ST:
                    dve.wait_ge(xroot, j + 1)
                    nc.vector.reciprocal(stat[:, 5, j:j + 1], stat[:, 4, j:j + 1]).then_inc(xrec, 1)
                    dve.wait_ge(xrec, j + 1)
                    if j >= 2:
                        dve.wait_ge(turned, j - 1)
                    nc.vector.scalar_tensor_tensor(out=scaled[:, j % 2, :], in0=x_tile(j), scalar=stat[:, 5, j:j + 1],
                                                   in1=g_pre[:], op0=ALU.mult, op1=ALU.mult).then_inc(xscaled, 1)
                j = i - lag
                if pre and 0 <= j < ST:
                    dve.wait_ge(hi_done, j + 1)
                    nc.vector.tensor_tensor(hT_lo[:, :, j * P:(j + 1) * P],
                                            tp[:, j % 2, :].rearrange("p (d s) -> p d s", d=DT),
                                            hT_hi[:, :, j * P:(j + 1) * P], ALU.subtract).then_inc(lo_done, 1)

        @block.tensor
        def _(pe):
            if not pre:
                return
            for i in range(ST):
                pe.wait_ge(xscaled, i + 1)
                if i >= 2:
                    pe.wait_ge(lo_done, i - 1)
                for d in range(DT):
                    last = nc.tensor.transpose(tp[:, i % 2, d * P:(d + 1) * P], scaled[:, i % 2, d * P:(d + 1) * P],
                                               ident[:])
                last.then_inc(turned, 1)


def setup_phase(nc, env, rel_table, rel_rows, rel_tiles):
    ident = env["ident"]
    with ExitStack() as ctx:
        table = ctx.enter_context(nc.sbuf_tensor("rel_in", [C_HEADS, 2 * REL_CLIP + 1], F32))
        rows = ctx.enter_context(nc.sbuf_tensor("rel_rows", [C_HEADS, REL_ROW], F32))
        s_load, s_id, s_rows = (phase_semaphore(nc, env, n) for n in ("rel_loaded", "ident_done", "rel_turned"))
        s_store = env["rel_stored"]
        width = C_BAND_COLS - REL_CLIP - 1
        block = ctx.enter_context(nc.Block())

        @block.sync
        def _(sp):
            sp.dma_start(table[:], rel_table).then_inc(s_load, 16)
            sp.wait_ge(s_rows, 2)
            sp.dma_start(rel_rows.ap(), rows[:]).then_inc(s_store, 16)
            sp.wait_ge(s_store, 16)
            sp.dma_start(rel_tiles.ap().rearrange("p h c -> h p c"),
                         bass.AP(rel_rows, P - 1, [[REL_ROW, C_HEADS], [-1, P], [1, C_BAND_COLS]]))\
                .then_inc(s_store, 16)

        @block.gpsimd
        def _(pool):
            nc.gpsimd.memset(ident[:], 0.0).then_inc(s_id, 1)
            pool.wait_ge(s_id, 1)
            nc.gpsimd.affine_select(out=ident[:], in_=ident[:], compare_op=ALU.not_equal, fill=1.0, base=0,
                                    pattern=[[-1, P]], channel_multiplier=1).then_inc(s_id, 1)

        @block.vector
        def _(dve):
            dve.wait_ge(s_load, 16)
            nc.vector.tensor_copy(rows[:, 0:width],
                                  table[:, 2 * REL_CLIP:2 * REL_CLIP + 1].broadcast_to([C_HEADS, width])).then_inc(s_rows, 1)
            nc.vector.tensor_copy(rows[:, width:REL_ROW], table[:, 2 * REL_CLIP + 1 - (REL_ROW - width):][:, ::-1])\
                .then_inc(s_rows, 1)


def mixer_phase(nc, kind, env, w_in, w_out, first_sum, small, rel_tiles=None):
    K = kind.name
    y, hT_hi, hT_lo, ident = env["y"], env["hT_hi"], env["hT_lo"], env["ident"]
    U = kind.units
    BW = {"A": SEQ, "B": 2 * P, "C": C_BAND_COLS}[K]
    EW = {"A": SEQ, "B": 2 * P, "C": C_BAND_COLS}[K]
    NB = {"A": 1, "B": B_HEADS, "C": 2}[K]
    R0 = {"A": 0, "B": 5, "C": 2}[K]
    w_view = w_in.rearrange("(t p) n -> p t n", p=P)
    with ExitStack() as ctx:
        def sb(name, shape, dt=F32):
            return ctx.enter_context(nc.sbuf_tensor(f"{K}_{name}", shape, dt))

        def ps(name, shape):
            return ctx.enter_context(nc.psum_tensor(f"{K}_{name}", shape, F32))

        def sem(name):
            return phase_semaphore(nc, env, f"{K}_{name}")

        w_f32 = sb("w_f32", [P, 2, D])
        w_hi = sb("w_hi", [P, 3, D], F32R)
        w_lo = sb("w_lo", [P, 3, D], F32R)
        q_st = sb("q_st", [P, 2, SEQ], F32R)
        k_hh = sb("k_hh", [P, 2, SEQ], F32R)
        k_ll = sb("k_ll", [P, 2, SEQ], F32R)
        v_st = sb("v_st", [P, 2, ST, P], F32R)
        vT = sb("vT", [P, SEQ])
        gate = sb("gate", [P, SEQ])
        o_sb = sb("o_sb", [P, SEQ])
        yT_hi = sb("yT_hi", [P, SEQ], F32R)
        yT_lo = sb("yT_lo", [P, SEQ], F32R)
        pT_hi = sb("pT_hi", [P, 8 - R0, 2 * P], F32R)
        pT_lo = sb("pT_lo", [P, 8 - R0, 2 * P], F32R)
        e_sb = sb("e_sb", [P, 4, EW])
        bias = sb("bias", [P, NB, BW])
        stats = sb("stats", [P, 5, 16])
        low, total, rec, sink_e, den = (stats[:, i, :] for i in range(5))
        dense = ps("dense", [P, 2, HALF])
        scores = ps("scores", [P, SEQ])
        turned = ps("turned", [P, SEQ])
        pv_ps = ps("pv_ps", [P, 2, HALF])

        w_loaded = {b: sem(f"w_loaded_{b}") for b in FILLS}
        w_hi_done = {b: sem(f"w_hi_done_{b}") for b in FILLS}
        w_ready = {b: sem(f"w_ready_{b}") for b in FILLS}
        filled = {b: sem(f"filled_{b}") for b in FILLS}
        hi_out = {b: sem(f"hi_out_{b}") for b in FILLS if b != "o"}
        drained = {b: sem(f"drained_{b}") for b in FILLS}
        s_scores, s_low, s_exp, s_rec, s_probs = (sem(n) for n in ("scored", "low_done", "exp_done", "rec_done", "probs"))
        s_turn, s_phi, s_plo, s_pv, s_pvc, s_out = (sem(n) for n in
                                                    ("turned_g", "p_hi", "p_lo", "pv_done", "pv_low", "out_part"))
        s_vturn, s_vhi, s_vlo, s_y, s_yhi, s_ylo = (sem(n) for n in
                                                    ("v_turned", "v_hi", "v_lo", "y_done", "y_hi", "y_lo"))
        s_zero, s_bias, s_const, s_passed = sem("zeroed"), sem("bias_ready"), sem("const_ready"), sem("passed")
        if K != "C":
            s_abs, s_bstep, s_mid = sem("abs_done"), sem("bias_step"), sem("mid_done")
        if K == "A":
            ones = sb("ones", [P, P])
            neg_lam, g_sub, eps = sb("neg_lam", [P, 1]), sb("g_sub", [P, 1]), sb("eps", [P, 1])
            lam_in, lam_prod, lam_sum = sb("lam_in", [P, 4, HD]), sb("lam_prod", [P, HD]), sb("lam_sum", [P, 4])
            s_sq, s_ssum, s_root, s_rroot, s_lam = (sem(n) for n in ("squared", "sq_summed", "root", "rroot", "lam_step"))
        if K == "B":
            sinks = sb("sinks", [P, 2, B_HEADS])
            s_sink, s_negsink = sem("sink_e"), sem("neg_sink")

        NS, NG, NP = kind.steps, kind.groups, kind.pvs
        LOOP = K == "C"

        def run_units(eng, unit):
            unit(0, True, False)
            if LOOP:
                with eng.Fori(1, U - 1) as u:
                    unit(u, False, False)
            else:
                for u in range(1, U - 1):
                    unit(u, False, False)
            unit(U - 1, False, True)

        def transposed_after(s):
            j = s - 2
            return kind.group_of_step(j) if 0 <= j < NS else None

        def pv_in(s):
            g = transposed_after(s - 1) if s >= 1 else None
            return g // 2 if g is not None and g % 2 else None

        def v_head(u, h):
            return u // 2 if K == "B" else h

        def e_of(j):
            return j % 4

        block = ctx.enter_context(nc.Block())

        @block.sync
        def _(sp):
            def settled(offset):
                return offset if isinstance(offset, int) else sp.snap(offset)

            def source(b, u):
                if b == "o":
                    return w_out[bass.ds(settled(kind.out_row + u * P), P), :]
                c0 = kind.cols[b] + (0 if K == "B" and b in "kv" else u * P)
                return w_view[:, :, bass.ds(settled(c0), P)]

            def load(b, src):
                slot = w_f32[:, STAGE_SLOT[b], :]
                sp.dma_start(slot if b == "o" else slot.rearrange("p (t n) -> p t n", t=DT), src)\
                    .then_inc(w_loaded[b], 16)

            def load_all(blocks, before):
                sources = [source(b, u) for b, u in blocks]
                for n, (b, u) in enumerate(blocks):
                    prev = previous_on(STAGE_SLOT, before, blocks, n)
                    if prev:
                        ge_apart(sp, s_passed, (w_ready[prev[0]], prev[1] + 1))
                    load(b, sources[n])

            def load_bias(u, wait):
                if wait:
                    sp.wait_ge(s_low, NS * u)
                sp.dma_start(bias[:], rel_tiles.ap()[:, bass.ds(2 * u, 2), :]).then_inc(s_const, 16)

            if K == "A":
                for i, name in enumerate(("q1", "k1", "q2", "k2")):
                    sp.dma_start(lam_in[:, i, :], small[name].partition_broadcast(P)).then_inc(s_const, 16)
                sp.dma_start(g_sub[:], small["g"].rearrange("(p a) -> p a", a=1)).then_inc(s_const, 16)
            if K == "B":
                sp.dma_start(sinks[:, 0, :], small["sinks"].partition_broadcast(P)).then_inc(s_const, 16)
            load_all([(b, 0) for b in kind.first], [])
            if K == "C":
                sp.wait_ge(env["rel_stored"], 32)
                load_bias(0, False)

            def unit(u, first, last):
                blocks = region1(kind, u, first, last) + region2(kind, u, last)
                if K == "C" and not first:
                    load_bias(u, True)
                load_all(blocks, blocks_before(kind, u, first))
            run_units(sp, unit)
            load_all([("o", U - 1)], region1(kind, U - 1, False, True))

        @block.gpsimd
        def _(pool):
            ts = nc.gpsimd.tensor_scalar

            def split(b, u, prev):
                ge_apart(pool, s_passed, (w_loaded[b], 16 * (u + 1)),
                         *([(filled[prev[0]], FILLS[prev[0]] * (prev[1] + 1))] if prev else []))
                src, hi = w_f32[:, STAGE_SLOT[b], :], w_hi[:, PART_SLOT[b], :]
                ts(hi, src, 1.0, 1.0, ALU.mult, ALU.mult).then_inc(w_hi_done[b], 1)
                pool.wait_ge(w_hi_done[b], u + 1)
                nc.gpsimd.tensor_tensor(w_lo[:, PART_SLOT[b], :], src, hi, ALU.subtract).then_inc(w_ready[b], 1)

            def split_all(blocks, before):
                for n, (b, u) in enumerate(blocks):
                    split(b, u, previous_on(PART_SLOT, before, blocks, n))

            def mask(tiles):
                n = tiles.shape[1]
                late = tiles[:, :, BW - CHUNK:BW]
                last = nc.gpsimd.affine_select(out=late, in_=late, compare_op=ALU.is_ge, fill=NEG, base=-CHUNK,
                                               pattern=[[0, n], [0, CHUNK]], channel_multiplier=1)
                if K != "A":
                    start = CHUNK if K == "B" else 0
                    early = tiles[:, :, start:start + CHUNK]
                    last = nc.gpsimd.affine_select(out=early, in_=early, compare_op=ALU.is_ge, fill=NEG, base=CHUNK - 1,
                                                   pattern=[[0, n], [0, CHUNK]], channel_multiplier=-1)
                if K == "B":
                    last = nc.gpsimd.memset(tiles[:, :, 0:CHUNK], NEG)
                return last

            def alibi(slot, n):
                b = bias[:, slot, :]
                nc.gpsimd.iota(b, pattern=[[-1, BW]], base=BW - P, channel_multiplier=1,
                               allow_small_or_imprecise_dtypes=True).then_inc(s_bstep, 1)
                pool.wait_ge(s_abs, n + 1)
                ts(b, b, -1.0, 1.0, ALU.mult, ALU.mult).then_inc(s_bstep, 1)
                pool.wait_ge(s_bstep, 2 * n + 2)
                mask(bias[:, slot:slot + 1, :]).then_inc(s_bias, 1)

            if first_sum:
                nc.gpsimd.memset(y[:], 0.0)
            nc.gpsimd.memset(pT_hi[:].bitcast(F32), 0.0).then_inc(s_zero, 1)
            nc.gpsimd.memset(pT_lo[:].bitcast(F32), 0.0).then_inc(s_zero, 1)
            if K == "A":
                nc.gpsimd.memset(ones[:], 1.0).then_inc(s_zero, 1)
                nc.gpsimd.memset(eps[:], EPS).then_inc(s_zero, 1)
            split_all([(b, 0) for b in kind.first], [])
            if K == "B":
                for h in range(B_HEADS):
                    alibi(h, h)

            def unit(u, first, last):
                if K == "A":
                    if not first:
                        pool.wait_ge(s_low, NS * u)
                    alibi(0, u)
                if K == "C":
                    ge_apart(pool, s_passed, (s_const, 16 * (u + 1)))
                    mask(bias[:]).then_inc(s_bias, 1)
                blocks = region1(kind, u, first, last) + region2(kind, u, last)
                split_all(blocks, blocks_before(kind, u, first))
            run_units(pool, unit)
            split_all([("o", U - 1)], region1(kind, U - 1, False, True))

        @block.tensor
        def _(pe):
            mm = nc.tensor.matmul

            def dense_mm(b, u, i, prev):
                per = MMS // FILLS[b]
                f, n = i // per, i % per
                bank = dense[:, f % 2, :]
                hi, lo = w_hi[:, PART_SLOT[b], :], w_lo[:, PART_SLOT[b], :]
                if i == 0:
                    ge(pe, w_ready[b], u + 1)
                    if b == "o":
                        ge(pe, s_ylo, u + 1)
                if n == 0 and prev is not None:
                    pb, pu, pf = prev
                    ge(pe, drained[pb], FILLS[pb] * pu + pf + 1)
                if b == "o":
                    s, half = f // 2, f % 2
                    lhs, rhs = ((yT_hi, hi), (yT_hi, lo), (yT_lo, hi))[n]
                    last = mm(bank, lhs[:, s * P:(s + 1) * P], rhs[:, half * HALF:(half + 1) * HALF],
                              start=n == 0, stop=n == per - 1)
                else:
                    d, part = n // 3, n % 3
                    lhs, rhs = ((hi, hT_hi), (hi, hT_lo), (lo, hT_hi))[part]
                    last = mm(bank, lhs[:, d * P:(d + 1) * P], rhs[:, d, f * HALF:(f + 1) * HALF],
                              start=n == 0, stop=n == per - 1)
                if n == per - 1:
                    last.then_inc(filled[b], 1)

            def dense_range(blocks, before, lo, hi):
                fills = fills_of(before)[-2:] + fills_of(blocks)
                for m in range(lo, hi):
                    b, u = blocks[m // MMS]
                    i = m % MMS
                    per = MMS // FILLS[b]
                    at = sum(FILLS[x] for x, _ in blocks[:m // MMS]) + i // per
                    at += len(fills) - sum(FILLS[x] for x, _ in blocks)
                    dense_mm(b, u, i, fills[at - 2] if at >= 2 else None)

            def turn_v(u):
                for s in range(ST):
                    last = nc.tensor.transpose(turned[:, s * P:(s + 1) * P], vT[:, s * P:(s + 1) * P], ident[:])
                last.then_inc(s_vturn, 1)

            def score(u, j):
                h, t = kind.step(j)
                kh = v_head(u, h)
                k0, n = kind.tiles(t)
                n1 = n * P if n <= 4 else {5: 256, 6: 384, 7: 384, 8: 512}[n]
                off = HALF - n1 if n > 4 else 0
                if j == 0:
                    ge(pe, drained["q"], 2 * (u + 1))
                    ge(pe, drained["k"], 2 * ((0 if K == "B" else u) + 1))
                ge(pe, s_low, NS * u + j)
                parts = [(off, k0 * P, n1)] + ([(HALF, k0 * P + n1, n * P - n1)] if n > 4 else [])
                for at, key, w in parts:
                    for i, k_part in enumerate((k_hh, k_ll)):
                        last = mm(scores[:, at:at + w], q_st[:, h, t * P:(t + 1) * P], k_part[:, kh, key:key + w],
                                  start=i == 0, stop=i == 1)
                last.then_inc(s_scores, 1)

            def turn(u, g):
                h, t = kind.group(g)
                e = e_of(2 * g) if K == "A" else e_of(g)
                n = kind.tiles(t)[1]
                ge(pe, s_probs, NG * u + g + 1)
                if g == 0:
                    ge(pe, s_vlo, (0 if K == "B" else u) + 1)
                ge(pe, s_plo, NG * u + g)
                for i in range(n):
                    last = nc.tensor.transpose(turned[:, i * P:(i + 1) * P], e_sb[:, e, i * P:(i + 1) * P], ident[:])
                last.then_inc(s_turn, 1)

            def times_v(u, n):
                h, t = kind.group(2 * n)
                vh = v_head(u, h)
                k0 = kind.tiles(t)[0]
                count = t + 2 - k0
                ge(pe, s_plo, NG * u + 2 * n + 2)
                ge(pe, s_out, NP * u + n - 1 if not isinstance(u, int) or NP * u + n > 1 else 0)
                out = pv_ps[:, n % 2, 0:2 * P]
                if K == "A" and n < 2:
                    ge(pe, s_root, u)
                if K == "A":
                    parts = ((0, pT_hi), (0, pT_lo), (1, pT_hi))
                else:
                    parts = ((vh, pT_hi), (vh, pT_lo))
                for i in range(count):
                    kt = k0 + i
                    r = kt - t + 6 - R0
                    for x, (which, p_part) in enumerate(parts):
                        last = mm(out, v_st[:, which, kt, :], p_part[:, r, :], start=i == 0 and x == 0,
                                  stop=i == count - 1 and x == len(parts) - 1)
                last.then_inc(s_pv, 1)

            def sub_norm(u):
                pe.wait_ge(s_sq, u + 1)
                pe.wait_ge(s_out, NP * (u + 1))
                for half in range(2):
                    last = mm(pv_ps[:, half, :], ones[:], e_sb[:, 0, half * HALF:(half + 1) * HALF], start=True, stop=True)
                last.then_inc(s_ssum, 1)

            pe.wait_ge(s_zero, 4 if K == "A" else 2)
            start = [(b, 0) for b in kind.first]
            dense_range(start, [], 0, MMS * len(start))
            pe.wait_ge(drained["v"], 2)
            turn_v(0)

            def unit(u, first, last):
                blocks = region1(kind, u, first, last) + region2(kind, u, last)
                before = blocks_before(kind, u, first)
                for s in range(NS + TAIL):
                    lo, hi = slice_of(kind, u, first, last, s)
                    dense_range(blocks, before, lo, hi)
                    if pv_in(s) is not None:
                        times_v(u, pv_in(s))
                    if transposed_after(s) is not None:
                        turn(u, transposed_after(s))
                    if s < NS:
                        score(u, s)
                if K == "A":
                    sub_norm(u)
                if not last and "v" in kind.per_unit:
                    ge(pe, drained["v"], 2 * (u + 2))
                    ge(pe, s_plo, NG * (u + 1))
                    turn_v(u + 1)
            run_units(pe, unit)
            dense_range([("o", U - 1)], region1(kind, U - 1, False, True), 0, MMS)

        @block.scalar
        def _(act):
            copy = nc.scalar.activation

            def hi_of_fill(b, u, f):
                if b == "o":
                    return
                act.wait_ge(filled[b], 2 * u + f + 1)
                bank, cols = dense[:, f % 2, :], slice(f * HALF, (f + 1) * HALF)
                if b == "g":
                    if not (isinstance(u, int) and u == 0):
                        act.wait_ge(s_y, u)
                    copy(gate[:, cols], bank, ACT.Tanh, scale=0.5).then_inc(hi_out[b], 1)
                if b == "v":
                    if not (isinstance(u, int) and u == 0):
                        act.wait_ge(s_vturn, u)
                    copy(vT[:, cols], bank, ACT.Copy).then_inc(drained[b], 1)
                if b == "q":
                    for h in range(2):
                        last = copy(q_st[0:HD, h, cols], bank[h * HD:(h + 1) * HD, :], ACT.Copy, scale=SCALE)
                    last.then_inc(hi_out[b], 1)
                if b == "k":
                    for h in range(2):
                        for half in range(2):
                            last = copy(k_hh[half * HD:(half + 1) * HD, h, cols], bank[h * HD:(h + 1) * HD, :], ACT.Copy)
                    last.then_inc(hi_out[b], 1)

            def exp(u, j):
                h, t = kind.step(j)
                n = kind.tiles(t)[1] * P
                e = e_sb[:, e_of(j), 0:n]
                ge(act, s_low, NS * u + j + 1)
                copy(e, e, ACT.Exp, scale=-1.0, bias=low[:, j:j + 1], accum_out=total[:, j:j + 1]).then_inc(s_exp, 1)
                if K == "B":
                    copy(sink_e[:, j:j + 1], low[:, j:j + 1], ACT.Exp,
                         bias=sinks[:, 0, 2 * u + h:2 * u + h + 1]).then_inc(s_sink, 1)

            def hi_of_group(u, g):
                h, t = kind.group(g)
                k0, n = kind.tiles(t)
                r = k0 - (t - t % 2) + 6 - R0
                ge(act, s_turn, NG * u + g + 1)
                if g % 2 == 0:
                    ge(act, s_pv, NP * u + g // 2)
                copy(pT_hi[:, r:r + n, (t % 2) * P:(t % 2 + 1) * P],
                     turned[:, 0:n * P].rearrange("p (n q) -> p n q", n=n), ACT.Copy).then_inc(s_phi, 1)

            def out_low(u, n):
                h, t = kind.group(2 * n)
                ge(act, s_pv, NP * u + n + 1)
                if n == 0:
                    ge(act, s_ylo, u)
                cols = slice(t * P, (t + 2) * P)
                if K == "A":
                    copy(o_sb[:, cols], pv_ps[:, n % 2, 0:2 * P], ACT.Copy).then_inc(s_out, 1)
                else:
                    copy(o_sb[h * HD:(h + 1) * HD, cols], pv_ps[HD:P, n % 2, 0:2 * P], ACT.Copy).then_inc(s_pvc, 1)

            def hi_of_v(u):
                ge(act, s_vturn, u + 1)
                if K == "A":
                    copy(v_st[:, 0, :, :], turned[:].rearrange("p (s f) -> p s f", s=ST), ACT.Copy).then_inc(s_vhi, 1)
                else:
                    copy(v_st[:, :, :, 0:HD], turned[:].rearrange("p (s h f) -> p h s f", s=ST, h=2), ACT.Copy)\
                        .then_inc(s_vhi, 1)

            act.wait_ge(s_zero, 4 if K == "A" else 2)
            if K == "A":
                act.wait_ge(s_lam, 2)
                copy(lam_sum[:, 2:4], lam_sum[:, 0:2], ACT.Exp).then_inc(s_lam, 1)
            if K == "B":
                act.wait_ge(s_const, 16)
            for b, f in [(b, f) for b in kind.first for f in range(2)]:
                hi_of_fill(b, 0, f)
            hi_of_v(0)
            if K == "B":
                for h in range(B_HEADS):
                    act.wait_ge(s_bstep, 2 * h + 1)
                    copy(bias[:, h, :], bias[:, h, :], ACT.Abs, scale=2.0 ** (-8.0 * (h + 1) / B_HEADS)).then_inc(s_abs, 1)

            def unit(u, first, last):
                if K == "A":
                    act.wait_ge(s_bstep, 2 * u + 1)
                    copy(bias[:, 0, :], bias[:, 0, :], ACT.Abs, scale=2.0 ** (-8.0 * (u + 1) / A_HEADS)).then_inc(s_abs, 1)
                for s in range(NS + TAIL):
                    g = transposed_after(s - 1) if s >= 1 else None
                    if g is not None:
                        hi_of_group(u, g)
                    if 1 <= s <= NS:
                        exp(u, s - 1)
                    for b, v, f in done_fills(kind, u, first, last, s):
                        hi_of_fill(b, v, f)
                    if pv_in(s) is not None:
                        out_low(u, pv_in(s))
                if K == "A":
                    ge(act, s_out, NP * (u + 1))
                    copy(e_sb[:, 0, :], o_sb[:], ACT.Square).then_inc(s_sq, 1)
                    act.wait_ge(s_ssum, u + 1)
                    copy(e_sb[:, 1, :].rearrange("p (a b) -> p a b", a=2), pv_ps[:], ACT.Sqrt, scale=1.0 / P,
                         bias=eps[:]).then_inc(s_root, 1)
                if not last and "v" in kind.per_unit:
                    hi_of_v(u + 1)
                ge(act, s_y, u + 1)
                ge(act, filled["o"], 16 * u if not (isinstance(u, int) and u == 0) else 0)
                copy(yT_hi[:], o_sb[:], ACT.Copy).then_inc(s_yhi, 1)
            run_units(act, unit)

        @block.vector
        def _(dve):
            tt, stt, ts = nc.vector.tensor_tensor, nc.vector.scalar_tensor_tensor, nc.vector.tensor_scalar

            def lo_of_fill(b, u, f):
                bank, cols = dense[:, f % 2, :], slice(f * HALF, (f + 1) * HALF)
                if b == "v":
                    return
                if b == "o":
                    dve.wait_ge(filled[b], 16 * u + f + 1)
                    into = y[:, f // 2, (f % 2) * HALF:(f % 2 + 1) * HALF]
                    ge(dve, drained[b], 16 * u)
                    tt(into, bank, into, ALU.add).then_inc(drained[b], 1)
                    return
                dve.wait_ge(hi_out[b], 2 * u + f + 1)
                if b == "g":
                    stt(out=gate[:, cols], in0=gate[:, cols], scalar=1.0, in1=bank, op0=ALU.add,
                        op1=ALU.mult).then_inc(drained[b], 1)
                if b == "q":
                    for h in range(2):
                        last = stt(out=q_st[HD:P, h, cols], in0=bank[h * HD:(h + 1) * HD, :], scalar=SCALE,
                                   in1=q_st[0:HD, h, cols], op0=ALU.mult, op1=ALU.subtract)
                    last.then_inc(drained[b], 1)
                if b == "k":
                    for h in range(2):
                        for half in range(2):
                            last = tt(k_ll[half * HD:(half + 1) * HD, h, cols], bank[h * HD:(h + 1) * HD, :],
                                      k_hh[0:HD, h, cols], ALU.subtract)
                    last.then_inc(drained[b], 1)

            def lowest(u, j):
                h, t = kind.step(j)
                n = kind.tiles(t)[1]
                n1 = n * P if n <= 4 else {5: 256, 6: 384, 7: 384, 8: 512}[n]
                off = HALF - n1 if n > 4 else 0
                n *= P
                slot = {"A": 0, "B": 2 * u + h if K == "B" else 0, "C": h}[K]
                g = (j - 4) // 2 if K == "A" else j - 4
                ge_apart(dve, s_passed, (s_scores, NS * u + j + 1),
                         (s_bias, (B_HEADS if K == "B" else u + 1) if j == 0 else 0),
                         (s_turn, NG * u + (g + 1 if j >= 4 else 0)))
                start = sinks[:, 1, 2 * u + h:2 * u + h + 1] if K == "B" else HUGE
                nc.vector.tensor_tensor_reduce(out=e_sb[:, e_of(j), 0:n], in0=scores[:, off:off + n],
                                               in1=bias[:, slot, BW - n:BW], scale=-1.0, scalar=start, op0=ALU.add,
                                               op1=ALU.min, accum_out=low[:, j:j + 1]).then_inc(s_low, 1)

            def normalise(u, j):
                h, t = kind.step(j)
                n = kind.tiles(t)[1] * P
                e = e_sb[:, e_of(j), 0:n]
                ge(dve, s_exp, NS * u + j + 1)
                src = total
                if K == "B":
                    dve.wait_ge(s_sink, NS * u + j + 1)
                    tt(den[:, j:j + 1], total[:, j:j + 1], sink_e[:, j:j + 1], ALU.add).then_inc(s_mid, 1)
                    dve.wait_ge(s_mid, NS * u + j + 1)
                    src = den
                nc.vector.reciprocal(rec[:, j:j + 1], src[:, j:j + 1]).then_inc(s_rec, 1)
                ge(dve, s_rec, NS * u + j + 1)
                if K != "A":
                    ts(e, e, rec[:, j:j + 1], None, ALU.mult).then_inc(s_probs, 1)
                elif h == 1:
                    e0 = e_sb[:, e_of(j - 1), 0:n]
                    ts(e, e, rec[:, j:j + 1], neg_lam[:], ALU.mult, ALU.mult).then_inc(s_mid, 1)
                    dve.wait_ge(s_mid, NG * u + j // 2 + 1)
                    stt(out=e0, in0=e0, scalar=rec[:, j - 1:j], in1=e, op0=ALU.mult, op1=ALU.add).then_inc(s_probs, 1)

            def lo_of_group(u, g):
                h, t = kind.group(g)
                k0, n = kind.tiles(t)
                r = k0 - (t - t % 2) + 6 - R0
                q = slice((t % 2) * P, (t % 2 + 1) * P)
                ge(dve, s_phi, NG * u + g + 1)
                tt(pT_lo[:, r:r + n, q], turned[:, 0:n * P].rearrange("p (n q) -> p n q", n=n), pT_hi[:, r:r + n, q],
                   ALU.subtract).then_inc(s_plo, 1)

            def out_sum(u, n):
                if K == "A":
                    return
                h, t = kind.group(2 * n)
                ge(dve, s_pvc, NP * u + n + 1)
                o = o_sb[h * HD:(h + 1) * HD, t * P:(t + 2) * P]
                tt(o, pv_ps[0:HD, n % 2, 0:2 * P], o, ALU.add).then_inc(s_out, 1)

            def lo_of_v(u):
                ge(dve, s_vhi, u + 1)
                if K == "A":
                    tt(v_st[:, 1, :, :], turned[:].rearrange("p (s f) -> p s f", s=ST), v_st[:, 0, :, :],
                       ALU.subtract).then_inc(s_vlo, 1)
                else:
                    tt(v_st[:, :, :, HD:P], turned[:].rearrange("p (s h f) -> p h s f", s=ST, h=2),
                       v_st[:, :, :, 0:HD], ALU.subtract).then_inc(s_vlo, 1)

            dve.wait_ge(s_zero, 4 if K == "A" else 2)
            if K == "A":
                dve.wait_ge(s_const, 80)
                for i in range(2):
                    nc.vector.tensor_tensor_reduce(out=lam_prod[:], in0=lam_in[:, 2 * i, :], in1=lam_in[:, 2 * i + 1, :],
                                                   scale=1.0, scalar=0.0, op0=ALU.mult, op1=ALU.add,
                                                   accum_out=lam_sum[:, i:i + 1]).then_inc(s_lam, 1)
                    dve.wait_ge(s_lam, i + 1)
                dve.wait_ge(s_lam, 3)
                stt(out=neg_lam[:], in0=lam_sum[:, 3:4], scalar=-LAM_INIT, in1=lam_sum[:, 2:3], op0=ALU.add,
                    op1=ALU.subtract).then_inc(s_lam, 1)
                ts(g_sub[:], g_sub[:], 0.5 * (1.0 - LAM_INIT), None, ALU.mult).then_inc(s_lam, 1)
                dve.wait_ge(s_lam, 5)
            if K == "B":
                dve.wait_ge(s_const, 16)
                ts(sinks[:, 1, :], sinks[:, 0, :], -1.0, None, ALU.mult).then_inc(s_negsink, 1)
                dve.wait_ge(s_negsink, 1)
            for b, f in [(b, f) for b in kind.first for f in range(2)]:
                lo_of_fill(b, 0, f)
            lo_of_v(0)

            def unit(u, first, last):
                for s in range(NS + TAIL):
                    if 0 <= s - 2 < NS:
                        normalise(u, s - 2)
                    g = transposed_after(s - 1) if s >= 1 else None
                    if g is not None:
                        lo_of_group(u, g)
                    if 1 <= s <= NS:
                        lowest(u, s - 1)
                    for b, v, f in done_fills(kind, u, first, last, s):
                        lo_of_fill(b, v, f)
                    if pv_in(s) is not None:
                        out_sum(u, pv_in(s))
                if K == "A":
                    root = e_sb[:, 1, :]
                    dve.wait_ge(s_root, u + 1)
                    nc.vector.reciprocal(root, root).then_inc(s_rroot, 1)
                    dve.wait_ge(s_rroot, 2 * u + 1)
                    tt(o_sb[:], o_sb[:], root, ALU.mult).then_inc(s_rroot, 1)
                    dve.wait_ge(s_rroot, 2 * u + 2)
                ge(dve, s_out, NP * (u + 1))
                ge(dve, drained["g"], 2 * (u + 1))
                stt(out=o_sb[:], in0=o_sb[:], scalar=g_sub[:] if K == "A" else 0.5, in1=gate[:], op0=ALU.mult,
                    op1=ALU.mult).then_inc(s_y, 1)
                if not last and "v" in kind.per_unit:
                    lo_of_v(u + 1)
                ge(dve, s_yhi, u + 1)
                tt(yT_lo[:], o_sb[:], yT_hi[:], ALU.subtract).then_inc(s_ylo, 1)

            run_units(dve, unit)
            for f in range(FILLS["o"]):
                lo_of_fill("o", U - 1, f)


def build(nc, x, pre_norm_g, post_norm_g, w_in_ab, w_out_ab, diff_lambda_q1, diff_lambda_k1, diff_lambda_q2,
          diff_lambda_k2, diff_subln_g, swa_sinks, w_in_c, w_out_c, rel_bias, out):
    rel_rows = nc.dram_tensor("rel_rows_dram", [C_HEADS, REL_ROW], F32, kind="Internal")
    rel_tiles = nc.dram_tensor("rel_tiles_dram", [P, C_HEADS, C_BAND_COLS], F32, kind="Internal")
    x1 = nc.dram_tensor("x1_dram", [SEQ, D], F32, kind="Internal")
    with ExitStack() as ctx:
        env = {
            "hT_hi": ctx.enter_context(nc.sbuf_tensor("hT_hi", [P, DT, SEQ], F32R)),
            "hT_lo": ctx.enter_context(nc.sbuf_tensor("hT_lo", [P, DT, SEQ], F32R)),
            "y": ctx.enter_context(nc.sbuf_tensor("y", [P, ST, D], F32)),
            "phase_semaphores": [],
            "rel_stored": ctx.enter_context(nc.semaphore("rel_stored")),
            "ident": ctx.enter_context(nc.sbuf_tensor("ident", [P, P], F32)),
        }
        setup_phase(nc, env, rel_bias[0], rel_rows, rel_tiles)
        norm_phase(nc, 0, env, x[0], None, None, pre_norm_g[0])
        mixer_phase(nc, KIND_A, env, w_in_ab[0], w_out_ab[0], True,
                    dict(q1=diff_lambda_q1[0], k1=diff_lambda_k1[0], q2=diff_lambda_q2[0], k2=diff_lambda_k2[0],
                         g=diff_subln_g[0]))
        mixer_phase(nc, KIND_B, env, w_in_ab[0], w_out_ab[0], False, dict(sinks=swa_sinks[0]))
        retire(nc, env)
        norm_phase(nc, 1, env, x[0], x1.ap(), post_norm_g[0], pre_norm_g[1])
        mixer_phase(nc, KIND_C, env, w_in_c[0], w_out_c[0], True, {}, rel_tiles)
        norm_phase(nc, 2, env, x1.ap(), out[0], post_norm_g[1], None)


INPUTS = ["x", "pre_norm_g", "post_norm_g", "w_in_ab", "w_out_ab", "diff_lambda_q1", "diff_lambda_k1", "diff_lambda_q2",
          "diff_lambda_k2", "diff_subln_g", "swa_sinks", "w_in_c", "w_out_c", "rel_bias"]


def kernel(**inputs):
    import concourse.bacc as bacc
    import numpy as np
    from concourse.bass_utils import run_bass_kernel_spmd

    nc = bacc.Bacc("TRN2", target_bir_lowering=False, num_devices=1, dynamic_dma_scratch_size=1024)
    arrays, aps = {}, {}
    for name in INPUTS:
        a = np.ascontiguousarray(inputs[name])
        arrays[f"in_{name}"] = a
        aps[name] = nc.dram_tensor(f"in_{name}", a.shape, mybir.dt.from_np(a.dtype), kind="ExternalInput").ap()
    out = nc.dram_tensor("out_x", (1, SEQ, D), F32, kind="ExternalOutput").ap()
    build(nc, out=out, **aps)
    r = run_bass_kernel_spmd(nc, [arrays], core_ids=[0])
    return r.results[0]["out_x"]
```

```python
import math
from contextlib import ExitStack

import concourse.bass as bass
from concourse import mybir
from concourse.alu_op_type import AluOpType as ALU

F32 = mybir.dt.float32
F32R = mybir.dt.float32r
ACT = mybir.ActivationFunctionType

P = 128
SEQ = 1024
D = 1024
ST = SEQ // P
DT = D // P
HALF = 512
HD = 64
CHUNK = 64
A_HEADS, B_HEADS, C_HEADS = 4, 8, 16
REL_CLIP = 256
C_BAND_COLS = 5 * P
REL_ROW = 768
EPS = 1e-6
NEG = -1e30
HUGE = 3e38
LAM_INIT = 0.8 - 0.6 * math.exp(-0.3 * 0)
SCALE = HD ** -0.5


class Kind:

    def __init__(self, name, units, cols, out_row, slopes, per_unit, ahead):
        self.name = name
        self.units = units
        self.cols = cols
        self.out_row = out_row
        self.first = ["v", "k", "q"]
        self.per_unit = per_unit
        self.ahead = ahead
        self.slopes = slopes
        self.steps = 16
        self.groups = 8 if name == "A" else 16
        self.pvs = self.groups // 2

    def tiles(self, t):
        first = {"A": 0, "B": max(0, t - 1), "C": max(0, t - 4)}[self.name]
        return first, t + 1 - first

    def step(self, j):
        return (j % 2, j // 2) if self.name == "A" else (j // 8, j % 8)

    def slope(self, u, h):
        if not self.slopes:
            return 1.0
        head = u if self.name == "A" else 2 * u + h
        return 2.0 ** (-8 * (head + 1) // self.slopes)

    def group_of_step(self, j):
        if self.name == "A":
            return j // 2 if j % 2 else None
        return j

    def group(self, g):
        return (0, g) if self.name == "A" else (g // 8, g % 8)


KIND_A = Kind("A", A_HEADS, dict(q=0, k=512, v=1024, g=2304), 0, A_HEADS, ["v"], ["k", "q"])
KIND_B = Kind("B", B_HEADS // 2, dict(q=1536, k=2048, v=2176, g=2816), 512, B_HEADS, [], ["q"])
KIND_C = Kind("C", C_HEADS // 2, dict(q=0, k=1024, v=2048, g=3072), 0, None, ["v"], ["k", "q"])

STAGE_SLOT = dict(o=0, k=0, g=1, v=1, q=1)
PART_SLOT = dict(o=0, k=1, g=1, v=2, q=2)
FILLS = dict(o=16, g=2, v=2, q=2, k=2)
MMS = 48


def blocks_of(kind, u, first, last):
    blocks = [("g", u)]
    if not first:
        blocks.append(("o", u - 1))
    if not last:
        blocks += [(b, u + 1) for b in kind.per_unit + kind.ahead]
    return blocks


def blocks_before(kind, u, first):
    if first:
        return [(b, 0) for b in kind.first]
    return blocks_of(kind, u - 1, False, False)


def previous_on(slot_map, before, blocks, n):
    for b, v in reversed(before + blocks[:n]):
        if slot_map[b] == slot_map[blocks[n][0]]:
            return b, v
    return None


def projections(blocks):
    return [(b, v) for b, v in blocks if b != "o"]


OUT_START = dict(A=3, B=2, C=2)
TAIL = 3


def slice_of(kind, u, first, last, s):
    n1 = MMS * (1 + (0 if last else len(kind.per_unit)))
    n2 = 0 if last else MMS * len(kind.ahead)
    if s < kind.steps:
        return n1 * s // kind.steps, n1 * (s + 1) // kind.steps
    t = s - kind.steps
    return n1 + n2 * t // TAIL, n1 + n2 * (t + 1) // TAIL


def done_fills(kind, u, first, last, s):
    lo, hi = slice_of(kind, u, first, last, s)
    out = []
    for n, (b, v) in enumerate(projections(blocks_of(kind, u, first, last))):
        for f in range(2):
            if lo < MMS * n + MMS // 2 * (f + 1) <= hi:
                out.append((b, v, f))
    return out


def out_fills(kind, first, s):
    if first or s < OUT_START[kind.name]:
        return range(0)
    span = kind.steps + TAIL - OUT_START[kind.name]
    t = s - OUT_START[kind.name]
    return range(-(-FILLS["o"] * t // span), -(-FILLS["o"] * (t + 1) // span))


def ge(eng, sem, value):
    if isinstance(value, int) and value <= 0:
        return
    eng.wait_ge(sem, value)


def ge_apart(eng, passed, *waits):
    for sem, value in waits:
        ge(eng, sem, value)
    if not all(isinstance(value, int) for _, value in waits):
        eng.sem_inc(passed, 1)


def phase_semaphore(nc, env, name):
    s = nc.alloc_semaphore(name)
    env["phase_semaphores"].append(s)
    return s


def retire(nc, env):
    nc.clear_and_free_semaphores(env["phase_semaphores"])
    env["phase_semaphores"] = []
    nc.all_engine_barrier()


def norm_phase(nc, layer, env, x_src, x_dst, post_g, pre_g):
    y, hT_hi, hT_lo, ident = env["y"], env["hT_hi"], env["hT_lo"], env["ident"]
    with ExitStack() as ctx:
        def sb(name, shape, dt=F32):
            return ctx.enter_context(nc.sbuf_tensor(f"n{layer}_{name}", shape, dt))

        def sem(name):
            return phase_semaphore(nc, env, f"n{layer}_{name}")

        xb = sb("xb", [P, 3, D])
        xn = sb("xn", [P, 3, D])
        scaled = sb("scaled", [P, 2, D])
        junk = sb("junk", [P, D])
        g_post = sb("g_post", [P, D])
        g_pre = sb("g_pre", [P, D])
        stat = sb("stat", [P, 6, ST])
        eps = sb("eps", [P, 1])
        tp = ctx.enter_context(nc.psum_tensor(f"n{layer}_tp", [P, 2, D], F32))
        x_loaded = [sem(f"x_loaded{i}") for i in range(3)]
        g_loaded, x_stored = sem("g_loaded"), [sem(f"x_stored{i}") for i in range(3)]
        consts, ysq, yroot, yrec, yscaled, xsum = (sem(n) for n in
                                                   ("consts", "ysq", "yroot", "yrec", "yscaled", "xsum"))
        xsq, xroot, xrec, xscaled, turned, hi_done, lo_done = (sem(n) for n in
                                                               ("xsq", "xroot", "xrec", "xscaled", "turned", "hi_done",
                                                                "lo_done"))
        post, pre = post_g is not None, pre_g is not None
        block = ctx.enter_context(nc.Block())
        lag = 2

        def x_tile(i):
            return xn[:, i % 3, :] if post else xb[:, i % 3, :]

        @block.sync
        def _(sp):
            if post:
                sp.dma_start(g_post[:], post_g.partition_broadcast(P)).then_inc(g_loaded, 16)
            if pre:
                sp.dma_start(g_pre[:], pre_g.partition_broadcast(P)).then_inc(g_loaded, 16)
            for i in range(ST + 1):
                if i < ST:
                    if i >= 3:
                        sp.wait_ge(xsum if post else xscaled, i - 2)
                        if not post:
                            sp.wait_ge(xsq, i - 2)
                    sp.dma_start(xb[:, i % 3, :], x_src[i * P:(i + 1) * P, :]).then_inc(x_loaded[i % 3], 16)
                if post and i >= 1:
                    sp.wait_ge(xsum, i)
                    sp.dma_start(x_dst[(i - 1) * P:i * P, :], xn[:, (i - 1) % 3, :]).then_inc(x_stored[(i - 1) % 3], 16)
            if post:
                for r in range(3):
                    sp.wait_ge(x_stored[r], 16 * ((ST - 1 - r) // 3 + 1))

        @block.gpsimd
        def _(pool):
            nc.gpsimd.memset(eps[:], EPS).then_inc(consts, 1)

        @block.scalar
        def _(act):
            act.wait_ge(consts, 1)
            for i in range(ST + lag):
                if post and i < ST:
                    nc.scalar.activation(junk[:], y[:, i, :], ACT.Square, accum_out=stat[:, 0, i:i + 1]).then_inc(ysq, 1)
                    act.wait_ge(ysq, i + 1)
                    nc.scalar.activation(stat[:, 1, i:i + 1], stat[:, 0, i:i + 1], ACT.Sqrt, scale=1.0 / D,
                                         bias=eps[:]).then_inc(yroot, 1)
                j = i - 1
                if pre and 0 <= j < ST:
                    if post:
                        act.wait_ge(xsum, j + 1)
                    else:
                        act.wait_ge(x_loaded[j % 3], 16 * (j // 3 + 1))
                    nc.scalar.activation(junk[:], x_tile(j), ACT.Square, accum_out=stat[:, 3, j:j + 1]).then_inc(xsq, 1)
                    act.wait_ge(xsq, j + 1)
                    nc.scalar.activation(stat[:, 4, j:j + 1], stat[:, 3, j:j + 1], ACT.Sqrt, scale=1.0 / D,
                                         bias=eps[:]).then_inc(xroot, 1)
                j = i - lag
                if pre and 0 <= j < ST:
                    act.wait_ge(turned, j + 1)
                    nc.scalar.activation(hT_hi[:, :, j * P:(j + 1) * P],
                                         tp[:, j % 2, :].rearrange("p (d s) -> p d s", d=DT), ACT.Copy).then_inc(hi_done, 1)

        @block.vector
        def _(dve):
            dve.wait_ge(g_loaded, 16 * (post + pre))
            for i in range(ST + lag):
                if post and i < ST:
                    dve.wait_ge(yroot, i + 1)
                    nc.vector.reciprocal(stat[:, 2, i:i + 1], stat[:, 1, i:i + 1]).then_inc(yrec, 1)
                    dve.wait_ge(yrec, i + 1)
                    if i >= 3:
                        dve.wait_ge(x_stored[i % 3], 16 * (i // 3))
                        if pre:
                            dve.wait_ge(xsq, i - 2)
                    nc.vector.scalar_tensor_tensor(out=xn[:, i % 3, :], in0=y[:, i, :], scalar=stat[:, 2, i:i + 1],
                                                   in1=g_post[:], op0=ALU.mult, op1=ALU.mult).then_inc(yscaled, 1)
                    dve.wait_ge(yscaled, i + 1)
                    dve.wait_ge(x_loaded[i % 3], 16 * (i // 3 + 1))
                    nc.vector.tensor_tensor(xn[:, i % 3, :], xn[:, i % 3, :], xb[:, i % 3, :], ALU.add).then_inc(xsum, 1)
                j = i - 1
                if pre and 0 <= j < ST:
                    dve.wait_ge(xroot, j + 1)
                    nc.vector.reciprocal(stat[:, 5, j:j + 1], stat[:, 4, j:j + 1]).then_inc(xrec, 1)
                    dve.wait_ge(xrec, j + 1)
                    if j >= 2:
                        dve.wait_ge(turned, j - 1)
                    nc.vector.scalar_tensor_tensor(out=scaled[:, j % 2, :], in0=x_tile(j), scalar=stat[:, 5, j:j + 1],
                                                   in1=g_pre[:], op0=ALU.mult, op1=ALU.mult).then_inc(xscaled, 1)
                j = i - lag
                if pre and 0 <= j < ST:
                    dve.wait_ge(hi_done, j + 1)
                    nc.vector.tensor_tensor(hT_lo[:, :, j * P:(j + 1) * P],
                                            tp[:, j % 2, :].rearrange("p (d s) -> p d s", d=DT),
                                            hT_hi[:, :, j * P:(j + 1) * P], ALU.subtract).then_inc(lo_done, 1)

        @block.tensor
        def _(pe):
            if not pre:
                return
            for i in range(ST):
                pe.wait_ge(xscaled, i + 1)
                if i >= 2:
                    pe.wait_ge(lo_done, i - 1)
                for d in range(DT):
                    last = nc.tensor.transpose(tp[:, i % 2, d * P:(d + 1) * P], scaled[:, i % 2, d * P:(d + 1) * P],
                                               ident[:])
                last.then_inc(turned, 1)


def setup_phase(nc, env, rel_table, rel_rows, rel_tiles):
    ident = env["ident"]
    with ExitStack() as ctx:
        table = ctx.enter_context(nc.sbuf_tensor("rel_in", [C_HEADS, 2 * REL_CLIP + 1], F32))
        rows = ctx.enter_context(nc.sbuf_tensor("rel_rows", [C_HEADS, REL_ROW], F32))
        s_load, s_id, s_rows = (phase_semaphore(nc, env, n) for n in ("rel_loaded", "ident_done", "rel_turned"))
        s_store = env["rel_stored"]
        width = C_BAND_COLS - REL_CLIP - 1
        block = ctx.enter_context(nc.Block())

        @block.sync
        def _(sp):
            sp.dma_start(table[:], rel_table).then_inc(s_load, 16)
            sp.wait_ge(s_rows, 2)
            sp.dma_start(rel_rows.ap(), rows[:]).then_inc(s_store, 16)
            sp.wait_ge(s_store, 16)
            sp.dma_start(rel_tiles.ap().rearrange("p h c -> h p c"),
                         bass.AP(rel_rows, P - 1, [[REL_ROW, C_HEADS], [-1, P], [1, C_BAND_COLS]]))\
                .then_inc(s_store, 16)

        @block.gpsimd
        def _(pool):
            nc.gpsimd.memset(ident[:], 0.0).then_inc(s_id, 1)
            pool.wait_ge(s_id, 1)
            nc.gpsimd.affine_select(out=ident[:], in_=ident[:], compare_op=ALU.not_equal, fill=1.0, base=0,
                                    pattern=[[-1, P]], channel_multiplier=1).then_inc(s_id, 1)

        @block.vector
        def _(dve):
            dve.wait_ge(s_load, 16)
            nc.vector.tensor_copy(rows[:, 0:width],
                                  table[:, 2 * REL_CLIP:2 * REL_CLIP + 1].broadcast_to([C_HEADS, width])).then_inc(s_rows, 1)
            nc.vector.tensor_copy(rows[:, width:REL_ROW], table[:, 2 * REL_CLIP + 1 - (REL_ROW - width):][:, ::-1])\
                .then_inc(s_rows, 1)


def mixer_phase(nc, kind, env, w_in, w_out, first_sum, small, rel_tiles=None):
    K = kind.name
    y, hT_hi, hT_lo, ident = env["y"], env["hT_hi"], env["hT_lo"], env["ident"]
    U = kind.units
    BW = {"A": SEQ, "B": 2 * P, "C": C_BAND_COLS}[K]
    EW = {"A": SEQ, "B": 2 * P, "C": C_BAND_COLS}[K]
    NB = {"A": 1, "B": 1, "C": 2}[K]
    R0 = {"A": 0, "B": 5, "C": 2}[K]
    w_view = w_in.rearrange("(t p) n -> p t n", p=P)
    with ExitStack() as ctx:
        def sb(name, shape, dt=F32):
            return ctx.enter_context(nc.sbuf_tensor(f"{K}_{name}", shape, dt))

        def ps(name, shape):
            return ctx.enter_context(nc.psum_tensor(f"{K}_{name}", shape, F32))

        def sem(name):
            return phase_semaphore(nc, env, f"{K}_{name}")

        w_f32 = sb("w_f32", [P, 2, D])
        w_hi = sb("w_hi", [P, 3, D], F32R)
        w_lo = sb("w_lo", [P, 3, D], F32R)
        q_st = sb("q_st", [P, 2, SEQ], F32R)
        k_hh = sb("k_hh", [P, 2, SEQ], F32R)
        k_l0 = sb("k_l0", [P, 2, SEQ], F32R)
        v_st = sb("v_st", [P, 2, ST, P], F32R)
        vT = sb("vT", [P, SEQ])
        gate = sb("gate", [P, SEQ])
        o_sb = sb("o_sb", [P, SEQ])
        yT_hi = sb("yT_hi", [P, SEQ], F32R)
        yT_lo = sb("yT_lo", [P, SEQ], F32R)
        pT_hi = sb("pT_hi", [P, 8 - R0, 2 * P], F32R)
        pT_lo = sb("pT_lo", [P, 8 - R0, 2 * P], F32R)
        e_sb = sb("e_sb", [P, 4, EW])
        bias = sb("bias", [P, NB, BW])
        stats = sb("stats", [P, 5, 16])
        low, total, rec, sink_e, den = (stats[:, i, :] for i in range(5))
        dense = ps("dense", [P, 3, HALF])
        scores = ps("scores", [P, SEQ])
        turned = ps("turned", [P, SEQ])
        pv_ps = ps("pv_ps", [P, 2, 2 * P])

        w_loaded = {b: sem(f"w_loaded_{b}") for b in FILLS}
        w_hi_done = {b: sem(f"w_hi_done_{b}") for b in FILLS}
        w_ready = {b: sem(f"w_ready_{b}") for b in FILLS}
        filled = {b: sem(f"filled_{b}") for b in FILLS}
        hi_out = {b: sem(f"hi_out_{b}") for b in FILLS if b != "o"}
        drained = {b: sem(f"drained_{b}") for b in FILLS}
        s_scores, s_low, s_exp, s_rec, s_probs = (sem(n) for n in ("scored", "low_done", "exp_done", "rec_done", "probs"))
        s_turn, s_phi, s_plo, s_pv, s_pvc, s_out = (sem(n) for n in
                                                    ("turned_g", "p_hi", "p_lo", "pv_done", "pv_low", "out_part"))
        s_vturn, s_vhi, s_vlo, s_y, s_yhi, s_ylo = (sem(n) for n in
                                                    ("v_turned", "v_hi", "v_lo", "y_done", "y_hi", "y_lo"))
        s_zero, s_bias, s_const, s_passed = sem("zeroed"), sem("bias_ready"), sem("const_ready"), sem("passed")
        if K != "C":
            s_abs, s_bstep, s_mid = sem("abs_done"), sem("bias_step"), sem("mid_done")
        if K == "A":
            ones, rms = sb("ones", [P, 1]), sb("rms", [P, 2, ST])
            neg_lam, g_sub, eps = sb("neg_lam", [P, 1]), sb("g_sub", [P, 1]), sb("eps", [P, 1])
            lam_in, lam_prod, lam_sum = sb("lam_in", [P, 4, HD]), sb("lam_prod", [P, HD]), sb("lam_sum", [P, 4])
            s_sq, s_ssum, s_root, s_rroot, s_lam = (sem(n) for n in ("squared", "sq_summed", "root", "rroot", "lam_step"))
        if K == "B":
            sinks = sb("sinks", [P, 2, B_HEADS])
            s_sink, s_negsink = sem("sink_e"), sem("neg_sink")

        NS, NG, NP = kind.steps, kind.groups, kind.pvs
        LOOP = K == "C"

        def run_units(eng, unit):
            unit(0, True, False)
            if LOOP:
                with eng.Fori(1, U - 1) as u:
                    unit(u, False, False)
            else:
                for u in range(1, U - 1):
                    unit(u, False, False)
            unit(U - 1, False, True)

        def transposed_after(s):
            j = s - 2
            return kind.group_of_step(j) if 0 <= j < NS else None

        def pv_in(s):
            g = transposed_after(s - 1) if s >= 1 else None
            return g // 2 if g is not None and g % 2 else None

        def v_head(u, h):
            return u // 2 if K == "B" else h

        def e_of(j):
            return j % 4

        block = ctx.enter_context(nc.Block())

        @block.sync
        def _(sp):
            def settled(offset):
                return offset if isinstance(offset, int) else sp.snap(offset)

            def source(b, u):
                if b == "o":
                    return w_out[bass.ds(settled(kind.out_row + u * P), P), :]
                c0 = kind.cols[b] + (0 if K == "B" and b in "kv" else u * P)
                return w_view[:, :, bass.ds(settled(c0), P)]

            def load(b, src):
                slot = w_f32[:, STAGE_SLOT[b], :]
                sp.dma_start(slot if b == "o" else slot.rearrange("p (t n) -> p t n", t=DT), src)\
                    .then_inc(w_loaded[b], 16)

            def load_all(blocks, before):
                sources = [source(b, u) for b, u in blocks]
                for n, (b, u) in enumerate(blocks):
                    prev = previous_on(STAGE_SLOT, before, blocks, n)
                    if prev:
                        ge_apart(sp, s_passed, (w_ready[prev[0]], prev[1] + 1))
                    load(b, sources[n])

            def load_bias(u, wait):
                if wait:
                    sp.wait_ge(s_low, NS * u)
                sp.dma_start(bias[:], rel_tiles.ap()[:, bass.ds(2 * u, 2), :]).then_inc(s_const, 16)

            if K == "A":
                for i, name in enumerate(("q1", "k1", "q2", "k2")):
                    sp.dma_start(lam_in[:, i, :], small[name].partition_broadcast(P)).then_inc(s_const, 16)
                sp.dma_start(g_sub[:], small["g"].rearrange("(p a) -> p a", a=1)).then_inc(s_const, 16)
            if K == "B":
                sp.dma_start(sinks[:, 0, :], small["sinks"].partition_broadcast(P)).then_inc(s_const, 16)
            load_all([(b, 0) for b in kind.first], [])
            if K == "C":
                sp.wait_ge(env["rel_stored"], 32)
                load_bias(0, False)

            def unit(u, first, last):
                blocks = blocks_of(kind, u, first, last)
                if K == "C" and not first:
                    load_bias(u, True)
                load_all(blocks, blocks_before(kind, u, first))
            run_units(sp, unit)
            load_all([("o", U - 1)], blocks_of(kind, U - 1, False, True))

        @block.gpsimd
        def _(pool):
            ts = nc.gpsimd.tensor_scalar

            def split(b, u, prev):
                ge_apart(pool, s_passed, (w_loaded[b], 16 * (u + 1)),
                         *([(filled[prev[0]], FILLS[prev[0]] * (prev[1] + 1))] if prev else []))
                src, hi = w_f32[:, STAGE_SLOT[b], :], w_hi[:, PART_SLOT[b], :]
                ts(hi, src, 1.0, 1.0, ALU.mult, ALU.mult).then_inc(w_hi_done[b], 1)
                pool.wait_ge(w_hi_done[b], u + 1)
                nc.gpsimd.tensor_tensor(w_lo[:, PART_SLOT[b], :], src, hi, ALU.subtract).then_inc(w_ready[b], 1)

            def split_all(blocks, before):
                for n, (b, u) in enumerate(blocks):
                    split(b, u, previous_on(PART_SLOT, before, blocks, n))

            def mask(tiles):
                n = tiles.shape[1]
                late = tiles[:, :, BW - CHUNK:BW]
                last = nc.gpsimd.affine_select(out=late, in_=late, compare_op=ALU.is_ge, fill=NEG, base=-CHUNK,
                                               pattern=[[0, n], [0, CHUNK]], channel_multiplier=1)
                if K != "A":
                    start = CHUNK if K == "B" else 0
                    early = tiles[:, :, start:start + CHUNK]
                    last = nc.gpsimd.affine_select(out=early, in_=early, compare_op=ALU.is_ge, fill=NEG, base=CHUNK - 1,
                                                   pattern=[[0, n], [0, CHUNK]], channel_multiplier=-1)
                if K == "B":
                    last = nc.gpsimd.memset(tiles[:, :, 0:CHUNK], NEG)
                return last

            def alibi():
                b = bias[:, 0, :]
                nc.gpsimd.iota(b, pattern=[[-1, BW]], base=BW - P, channel_multiplier=1,
                               allow_small_or_imprecise_dtypes=True).then_inc(s_bstep, 1)
                pool.wait_ge(s_abs, 1)
                ts(b, b, -1.0, 1.0, ALU.mult, ALU.mult).then_inc(s_bstep, 1)
                pool.wait_ge(s_bstep, 2)
                mask(bias[:]).then_inc(s_bias, 1)

            if first_sum:
                nc.gpsimd.memset(y[:], 0.0)
            nc.gpsimd.memset(pT_hi[:].bitcast(F32), 0.0).then_inc(s_zero, 1)
            nc.gpsimd.memset(pT_lo[:].bitcast(F32), 0.0).then_inc(s_zero, 1)
            nc.gpsimd.memset(k_l0[:].bitcast(F32), 0.0).then_inc(s_zero, 1)
            if K == "A":
                nc.gpsimd.memset(ones[:], 1.0).then_inc(s_zero, 1)
                nc.gpsimd.memset(eps[:], EPS).then_inc(s_zero, 1)
            split_all([(b, 0) for b in kind.first], [])
            if K != "C":
                alibi()

            def unit(u, first, last):
                blocks, before = blocks_of(kind, u, first, last), blocks_before(kind, u, first)
                split(*blocks[0], previous_on(PART_SLOT, before, blocks, 0))
                if K == "C":
                    ge_apart(pool, s_passed, (s_const, 16 * (u + 1)))
                    mask(bias[:]).then_inc(s_bias, 1)
                for n in range(1, len(blocks)):
                    split(*blocks[n], previous_on(PART_SLOT, before, blocks, n))
            run_units(pool, unit)
            split("o", U - 1, ("o", U - 2))

        @block.tensor
        def _(pe):
            mm = nc.tensor.matmul

            def project(blocks, last_before, lo, hi):
                for m in range(lo, hi):
                    n, i = m // MMS, m % MMS
                    b, u = blocks[n]
                    f, d, part = i // (MMS // 2), i % (MMS // 2) // 3, i % 3
                    w, w_l = w_hi[:, PART_SLOT[b], :], w_lo[:, PART_SLOT[b], :]
                    if i == 0:
                        ge(pe, w_ready[b], u + 1)
                    if i % (MMS // 2) == 0:
                        pb, pu = blocks[n - 1] if n else last_before if last_before else (None, 0)
                        if pb:
                            ge(pe, drained[pb], 2 * pu + f + 1)
                    lhs, rhs = ((w, hT_hi), (w, hT_lo), (w_l, hT_hi))[part]
                    last = mm(dense[:, f, :], lhs[:, d * P:(d + 1) * P], rhs[:, d, f * HALF:(f + 1) * HALF],
                              start=d == 0 and part == 0, stop=d == DT - 1 and part == 2)
                    if d == DT - 1 and part == 2:
                        last.then_inc(filled[b], 1)

            def project_out(u, f):
                s, half = f // 2, f % 2
                if f == 0:
                    ge(pe, w_ready["o"], u + 1)
                    ge(pe, s_ylo, u + 1)
                    if K == "A":
                        ge(pe, s_root, u + 1)
                ge(pe, drained["o"], FILLS["o"] * u + f)
                w, w_l = w_hi[:, PART_SLOT["o"], :], w_lo[:, PART_SLOT["o"], :]
                for n, (lhs, rhs) in enumerate(((yT_hi, w), (yT_hi, w_l), (yT_lo, w))):
                    last = mm(dense[:, 2, :], lhs[:, s * P:(s + 1) * P], rhs[:, half * HALF:(half + 1) * HALF],
                              start=n == 0, stop=n == 2)
                last.then_inc(filled["o"], 1)

            def turn_v(u):
                for s in range(ST):
                    last = nc.tensor.transpose(turned[:, s * P:(s + 1) * P], vT[:, s * P:(s + 1) * P], ident[:])
                last.then_inc(s_vturn, 1)

            def score(u, j):
                h, t = kind.step(j)
                kh = v_head(u, h)
                k0, n = kind.tiles(t)
                n1 = n * P if n <= 4 else {5: 256, 6: 384, 7: 384, 8: 512}[n]
                off = HALF - n1 if n > 4 else 0
                if j == 0:
                    ge(pe, drained["q"], 2 * (u + 1))
                    ge(pe, drained["k"], 2 * ((0 if K == "B" else u) + 1))
                ge(pe, s_low, NS * u + j)
                parts = [(off, k0 * P, n1)] + ([(HALF, k0 * P + n1, n * P - n1)] if n > 4 else [])
                for at, key, w in parts:
                    for i, k_part in enumerate((k_hh, k_l0)):
                        last = mm(scores[:, at:at + w], q_st[:, h, t * P:(t + 1) * P], k_part[:, kh, key:key + w],
                                  start=i == 0, stop=i == 1)
                last.then_inc(s_scores, 1)

            def turn(u, g):
                h, t = kind.group(g)
                e = e_of(2 * g) if K == "A" else e_of(g)
                n = kind.tiles(t)[1]
                ge(pe, s_probs, NG * u + g + 1)
                if g == 0:
                    ge(pe, s_vlo, (0 if K == "B" else u) + 1)
                ge(pe, s_plo, NG * u + g)
                for i in range(n):
                    last = nc.tensor.transpose(turned[:, i * P:(i + 1) * P], e_sb[:, e, i * P:(i + 1) * P], ident[:])
                last.then_inc(s_turn, 1)

            def times_v(u, n):
                h, t = kind.group(2 * n)
                vh = v_head(u, h)
                k0 = kind.tiles(t)[0]
                count = t + 2 - k0
                ge(pe, s_plo, NG * u + 2 * n + 2)
                ge(pe, s_out, NP * u + n - 1 if not isinstance(u, int) or NP * u + n > 1 else 0)
                out = pv_ps[:, n % 2, :]
                if K == "A":
                    parts = ((0, pT_hi), (0, pT_lo), (1, pT_hi))
                else:
                    parts = ((vh, pT_hi), (vh, pT_lo))
                for i in range(count):
                    kt = k0 + i
                    r = kt - t + 6 - R0
                    for x, (which, p_part) in enumerate(parts):
                        last = mm(out, v_st[:, which, kt, :], p_part[:, r, :], start=i == 0 and x == 0,
                                  stop=i == count - 1 and x == len(parts) - 1)
                last.then_inc(s_pv, 1)

            def square_sums(u):
                ge(pe, s_sq, u + 1)
                ge(pe, drained["o"], FILLS["o"] * u)
                for t in range(ST):
                    last = mm(dense[:, 2, t:t + 1], vT[:, t * P:(t + 1) * P], ones[:], start=True, stop=True)
                last.then_inc(s_ssum, 1)

            pe.wait_ge(s_zero, 5 if K == "A" else 3)
            start = [(b, 0) for b in kind.first]
            project(start, None, 0, MMS)
            pe.wait_ge(drained["v"], 2)
            turn_v(0)
            project(start, None, MMS, MMS * len(start))

            def unit(u, first, last):
                blocks = projections(blocks_of(kind, u, first, last))
                before = projections(blocks_before(kind, u, first))[-1]
                for s in range(NS + TAIL):
                    lo, hi = slice_of(kind, u, first, last, s)
                    fills = out_fills(kind, first, s)
                    if len(fills) > 1:
                        project_out(u - 1, fills[0])
                    project(blocks, before, lo, hi)
                    if K == "A" and s == 1 and not first:
                        square_sums(u - 1)
                    if len(fills) > 0:
                        project_out(u - 1, fills[-1])
                    if pv_in(s) is not None:
                        times_v(u, pv_in(s))
                    if transposed_after(s) is not None:
                        turn(u, transposed_after(s))
                    if s < NS:
                        score(u, s)
                if not last and "v" in kind.per_unit:
                    ge(pe, drained["v"], 2 * (u + 2))
                    ge(pe, s_plo, NG * (u + 1))
                    turn_v(u + 1)
            run_units(pe, unit)
            if K == "A":
                square_sums(U - 1)
            for f in range(FILLS["o"]):
                project_out(U - 1, f)

        @block.scalar
        def _(act):
            copy = nc.scalar.activation

            def hi_of_fill(b, u, f):
                act.wait_ge(filled[b], 2 * u + f + 1)
                bank, cols = dense[:, f, :], slice(f * HALF, (f + 1) * HALF)
                if b == "g":
                    if not (isinstance(u, int) and u == 0):
                        act.wait_ge(s_y, u)
                    copy(gate[:, cols], bank, ACT.Tanh, scale=0.5).then_inc(hi_out[b], 1)
                if b == "v":
                    if not (isinstance(u, int) and u == 0):
                        act.wait_ge(s_vturn, u)
                    copy(vT[:, cols], bank, ACT.Copy).then_inc(drained[b], 1)
                if b == "q":
                    for h in range(2):
                        last = copy(q_st[0:HD, h, cols], bank[h * HD:(h + 1) * HD, :], ACT.Copy,
                                    scale=SCALE / kind.slope(u, h))
                    last.then_inc(hi_out[b], 1)
                if b == "k":
                    for h in range(2):
                        for half in range(2):
                            last = copy(k_hh[half * HD:(half + 1) * HD, h, cols], bank[h * HD:(h + 1) * HD, :], ACT.Copy)
                    last.then_inc(hi_out[b], 1)

            def exp(u, j):
                h, t = kind.step(j)
                n = kind.tiles(t)[1] * P
                e = e_sb[:, e_of(j), 0:n]
                ge(act, s_low, NS * u + j + 1)
                copy(e, e, ACT.Exp, scale=-1.0, bias=low[:, j:j + 1], accum_out=total[:, j:j + 1]).then_inc(s_exp, 1)
                if K == "B":
                    copy(sink_e[:, j:j + 1], low[:, j:j + 1], ACT.Exp,
                         bias=sinks[:, 0, 2 * u + h:2 * u + h + 1]).then_inc(s_sink, 1)

            def hi_of_group(u, g):
                h, t = kind.group(g)
                k0, n = kind.tiles(t)
                r = k0 - (t - t % 2) + 6 - R0
                ge(act, s_turn, NG * u + g + 1)
                if g % 2 == 0:
                    ge(act, s_pv, NP * u + g // 2)
                copy(pT_hi[:, r:r + n, (t % 2) * P:(t % 2 + 1) * P],
                     turned[:, 0:n * P].rearrange("p (n q) -> p n q", n=n), ACT.Copy).then_inc(s_phi, 1)

            def out_low(u, n):
                h, t = kind.group(2 * n)
                ge(act, s_pv, NP * u + n + 1)
                if n == 0:
                    ge(act, s_ylo, u)
                cols = slice(t * P, (t + 2) * P)
                if K == "A":
                    copy(o_sb[:, cols], pv_ps[:, n % 2, :], ACT.Copy).then_inc(s_out, 1)
                else:
                    copy(o_sb[h * HD:(h + 1) * HD, cols], pv_ps[HD:P, n % 2, :], ACT.Copy).then_inc(s_pvc, 1)

            def hi_of_v(u):
                ge(act, s_vturn, u + 1)
                if K == "A":
                    copy(v_st[:, 0, :, :], turned[:].rearrange("p (s f) -> p s f", s=ST), ACT.Copy).then_inc(s_vhi, 1)
                else:
                    copy(v_st[:, :, :, 0:HD], turned[:].rearrange("p (s h f) -> p h s f", s=ST, h=2), ACT.Copy)\
                        .then_inc(s_vhi, 1)

            act.wait_ge(s_zero, 5 if K == "A" else 3)
            if K == "A":
                act.wait_ge(s_lam, 2)
                copy(lam_sum[:, 2:4], lam_sum[:, 0:2], ACT.Exp).then_inc(s_lam, 1)
            if K == "B":
                act.wait_ge(s_const, 16)
            for b, f in [(b, f) for b in kind.first for f in range(2)]:
                hi_of_fill(b, 0, f)
                if (b, f) == ("v", 1):
                    hi_of_v(0)
            if K != "C":
                act.wait_ge(s_bstep, 1)
                copy(bias[:], bias[:], ACT.Abs).then_inc(s_abs, 1)

            def root_mean(u):
                act.wait_ge(s_ssum, u + 1)
                ge(act, drained["o"], FILLS["o"] * u)
                copy(rms[:, 0, :], dense[:, 2, 0:ST], ACT.Sqrt, scale=1.0 / P, bias=eps[:]).then_inc(s_root, 1)

            def unit(u, first, last):
                for s in range(NS + TAIL):
                    g = transposed_after(s - 1) if s >= 1 else None
                    if g is not None:
                        hi_of_group(u, g)
                    if 1 <= s <= NS:
                        exp(u, s - 1)
                    for b, v, f in done_fills(kind, u, first, last, s):
                        hi_of_fill(b, v, f)
                    if pv_in(s) is not None:
                        out_low(u, pv_in(s))
                    if K == "A" and s == 1 and not first:
                        root_mean(u - 1)
                if not last and "v" in kind.per_unit:
                    hi_of_v(u + 1)
                if K == "A":
                    ge(act, s_out, NP * (u + 1))
                    copy(vT[:], o_sb[:], ACT.Square).then_inc(s_sq, 1)
                ge(act, s_y, u + 1)
                ge(act, filled["o"], FILLS["o"] * u)
                copy(yT_hi[:], o_sb[:], ACT.Copy).then_inc(s_yhi, 1)
            run_units(act, unit)
            if K == "A":
                root_mean(U - 1)

        @block.vector
        def _(dve):
            tt, stt, ts = nc.vector.tensor_tensor, nc.vector.scalar_tensor_tensor, nc.vector.tensor_scalar

            def lo_of_fill(b, u, f):
                bank, cols = dense[:, f, :], slice(f * HALF, (f + 1) * HALF)
                if b == "v":
                    return
                dve.wait_ge(hi_out[b], 2 * u + f + 1)
                if b == "g":
                    stt(out=gate[:, cols], in0=gate[:, cols], scalar=1.0, in1=bank, op0=ALU.add,
                        op1=ALU.mult).then_inc(drained[b], 1)
                if b == "q":
                    for h in range(2):
                        last = stt(out=q_st[HD:P, h, cols], in0=bank[h * HD:(h + 1) * HD, :],
                                   scalar=SCALE / kind.slope(u, h), in1=q_st[0:HD, h, cols], op0=ALU.mult, op1=ALU.subtract)
                    last.then_inc(drained[b], 1)
                if b == "k":
                    for h in range(2):
                        last = tt(k_l0[0:HD, h, cols], bank[h * HD:(h + 1) * HD, :], k_hh[0:HD, h, cols], ALU.subtract)
                    last.then_inc(drained[b], 1)

            def add_out(u, f):
                dve.wait_ge(filled["o"], FILLS["o"] * u + f + 1)
                if f == 0:
                    ge(dve, drained["o"], FILLS["o"] * u)
                    if K == "A":
                        dve.wait_ge(s_root, u + 1)
                        nc.vector.reciprocal(rms[:, 1, :], rms[:, 0, :]).then_inc(s_rroot, 1)
                        dve.wait_ge(s_rroot, u + 1)
                into = y[:, f // 2, (f % 2) * HALF:(f % 2 + 1) * HALF]
                if K == "A":
                    stt(out=into, in0=dense[:, 2, :], scalar=rms[:, 1, f // 2:f // 2 + 1], in1=into, op0=ALU.mult,
                        op1=ALU.add).then_inc(drained["o"], 1)
                else:
                    tt(into, dense[:, 2, :], into, ALU.add).then_inc(drained["o"], 1)

            def lowest(u, j):
                h, t = kind.step(j)
                n = kind.tiles(t)[1]
                n1 = n * P if n <= 4 else {5: 256, 6: 384, 7: 384, 8: 512}[n]
                off = HALF - n1 if n > 4 else 0
                n *= P
                slot = h if K == "C" else 0
                g = (j - 4) // 2 if K == "A" else j - 4
                ge_apart(dve, s_passed, (s_scores, NS * u + j + 1),
                         (s_bias, (u if K == "C" else 0) + 1 if j == 0 else 0),
                         (s_turn, NG * u + (g + 1 if j >= 4 else 0)))
                start = sinks[:, 1, 2 * u + h:2 * u + h + 1] if K == "B" else HUGE
                nc.vector.tensor_tensor_reduce(out=e_sb[:, e_of(j), 0:n], in0=scores[:, off:off + n],
                                               in1=bias[:, slot, BW - n:BW], scale=-kind.slope(u, h), scalar=start, op0=ALU.add,
                                               op1=ALU.min, accum_out=low[:, j:j + 1]).then_inc(s_low, 1)

            def normalise(u, j):
                h, t = kind.step(j)
                n = kind.tiles(t)[1] * P
                e = e_sb[:, e_of(j), 0:n]
                ge(dve, s_exp, NS * u + j + 1)
                src = total
                if K == "B":
                    dve.wait_ge(s_sink, NS * u + j + 1)
                    tt(den[:, j:j + 1], total[:, j:j + 1], sink_e[:, j:j + 1], ALU.add).then_inc(s_mid, 1)
                    dve.wait_ge(s_mid, NS * u + j + 1)
                    src = den
                nc.vector.reciprocal(rec[:, j:j + 1], src[:, j:j + 1]).then_inc(s_rec, 1)
                ge(dve, s_rec, NS * u + j + 1)
                if K != "A":
                    ts(e, e, rec[:, j:j + 1], None, ALU.mult).then_inc(s_probs, 1)
                elif h == 1:
                    e0 = e_sb[:, e_of(j - 1), 0:n]
                    ts(e, e, rec[:, j:j + 1], neg_lam[:], ALU.mult, ALU.mult).then_inc(s_mid, 1)
                    dve.wait_ge(s_mid, NG * u + j // 2 + 1)
                    stt(out=e0, in0=e0, scalar=rec[:, j - 1:j], in1=e, op0=ALU.mult, op1=ALU.add).then_inc(s_probs, 1)

            def lo_of_group(u, g):
                h, t = kind.group(g)
                k0, n = kind.tiles(t)
                r = k0 - (t - t % 2) + 6 - R0
                q = slice((t % 2) * P, (t % 2 + 1) * P)
                ge(dve, s_phi, NG * u + g + 1)
                tt(pT_lo[:, r:r + n, q], turned[:, 0:n * P].rearrange("p (n q) -> p n q", n=n), pT_hi[:, r:r + n, q],
                   ALU.subtract).then_inc(s_plo, 1)

            def out_sum(u, n):
                if K == "A":
                    return
                h, t = kind.group(2 * n)
                ge(dve, s_pvc, NP * u + n + 1)
                o = o_sb[h * HD:(h + 1) * HD, t * P:(t + 2) * P]
                tt(o, pv_ps[0:HD, n % 2, :], o, ALU.add).then_inc(s_out, 1)

            def lo_of_v(u):
                ge(dve, s_vhi, u + 1)
                if K == "A":
                    tt(v_st[:, 1, :, :], turned[:].rearrange("p (s f) -> p s f", s=ST), v_st[:, 0, :, :],
                       ALU.subtract).then_inc(s_vlo, 1)
                else:
                    tt(v_st[:, :, :, HD:P], turned[:].rearrange("p (s h f) -> p h s f", s=ST, h=2),
                       v_st[:, :, :, 0:HD], ALU.subtract).then_inc(s_vlo, 1)

            dve.wait_ge(s_zero, 5 if K == "A" else 3)
            if K == "A":
                dve.wait_ge(s_const, 80)
                for i in range(2):
                    nc.vector.tensor_tensor_reduce(out=lam_prod[:], in0=lam_in[:, 2 * i, :], in1=lam_in[:, 2 * i + 1, :],
                                                   scale=1.0, scalar=0.0, op0=ALU.mult, op1=ALU.add,
                                                   accum_out=lam_sum[:, i:i + 1]).then_inc(s_lam, 1)
                    dve.wait_ge(s_lam, i + 1)
                dve.wait_ge(s_lam, 3)
                stt(out=neg_lam[:], in0=lam_sum[:, 3:4], scalar=-LAM_INIT, in1=lam_sum[:, 2:3], op0=ALU.add,
                    op1=ALU.subtract).then_inc(s_lam, 1)
                ts(g_sub[:], g_sub[:], 0.5 * (1.0 - LAM_INIT), None, ALU.mult).then_inc(s_lam, 1)
                dve.wait_ge(s_lam, 5)
            if K == "B":
                dve.wait_ge(s_const, 16)
                ts(sinks[:, 1, :], sinks[:, 0, :], -1.0, None, ALU.mult).then_inc(s_negsink, 1)
                dve.wait_ge(s_negsink, 1)
            lo_of_v(0)
            for b, f in [(b, f) for b in kind.first for f in range(2)]:
                lo_of_fill(b, 0, f)

            def gated_lo(u):
                ge(dve, s_yhi, u + 1)
                tt(yT_lo[:], o_sb[:], yT_hi[:], ALU.subtract).then_inc(s_ylo, 1)

            def unit(u, first, last):
                for s in range(NS + TAIL):
                    if 0 <= s - 2 < NS:
                        normalise(u, s - 2)
                    g = transposed_after(s - 1) if s >= 1 else None
                    if g is not None:
                        lo_of_group(u, g)
                    if 1 <= s <= NS:
                        lowest(u, s - 1)
                    if s == 1 and not first:
                        gated_lo(u - 1)
                    fills = out_fills(kind, first, s)
                    if len(fills) > 1:
                        add_out(u - 1, fills[0])
                    for b, v, f in done_fills(kind, u, first, last, s):
                        lo_of_fill(b, v, f)
                    if len(fills) > 0:
                        add_out(u - 1, fills[-1])
                    if pv_in(s) is not None:
                        out_sum(u, pv_in(s))
                ge(dve, s_out, NP * (u + 1))
                ge(dve, drained["g"], 2 * (u + 1))
                if K == "A":
                    ge(dve, s_sq, u + 1)
                stt(out=o_sb[:], in0=o_sb[:], scalar=g_sub[:] if K == "A" else 0.5, in1=gate[:], op0=ALU.mult,
                    op1=ALU.mult).then_inc(s_y, 1)
                if not last and "v" in kind.per_unit:
                    lo_of_v(u + 1)

            run_units(dve, unit)
            gated_lo(U - 1)
            for f in range(FILLS["o"]):
                add_out(U - 1, f)


def build(nc, x, pre_norm_g, post_norm_g, w_in_ab, w_out_ab, diff_lambda_q1, diff_lambda_k1, diff_lambda_q2,
          diff_lambda_k2, diff_subln_g, swa_sinks, w_in_c, w_out_c, rel_bias, out):
    rel_rows = nc.dram_tensor("rel_rows_dram", [C_HEADS, REL_ROW], F32, kind="Internal")
    rel_tiles = nc.dram_tensor("rel_tiles_dram", [P, C_HEADS, C_BAND_COLS], F32, kind="Internal")
    x1 = nc.dram_tensor("x1_dram", [SEQ, D], F32, kind="Internal")
    with ExitStack() as ctx:
        env = {
            "hT_hi": ctx.enter_context(nc.sbuf_tensor("hT_hi", [P, DT, SEQ], F32R)),
            "hT_lo": ctx.enter_context(nc.sbuf_tensor("hT_lo", [P, DT, SEQ], F32R)),
            "y": ctx.enter_context(nc.sbuf_tensor("y", [P, ST, D], F32)),
            "phase_semaphores": [],
            "rel_stored": ctx.enter_context(nc.semaphore("rel_stored")),
            "ident": ctx.enter_context(nc.sbuf_tensor("ident", [P, P], F32)),
        }
        setup_phase(nc, env, rel_bias[0], rel_rows, rel_tiles)
        norm_phase(nc, 0, env, x[0], None, None, pre_norm_g[0])
        mixer_phase(nc, KIND_A, env, w_in_ab[0], w_out_ab[0], True,
                    dict(q1=diff_lambda_q1[0], k1=diff_lambda_k1[0], q2=diff_lambda_q2[0], k2=diff_lambda_k2[0],
                         g=diff_subln_g[0]))
        mixer_phase(nc, KIND_B, env, w_in_ab[0], w_out_ab[0], False, dict(sinks=swa_sinks[0]))
        retire(nc, env)
        norm_phase(nc, 1, env, x[0], x1.ap(), post_norm_g[0], pre_norm_g[1])
        mixer_phase(nc, KIND_C, env, w_in_c[0], w_out_c[0], True, {}, rel_tiles)
        norm_phase(nc, 2, env, x1.ap(), out[0], post_norm_g[1], None)


INPUTS = ["x", "pre_norm_g", "post_norm_g", "w_in_ab", "w_out_ab", "diff_lambda_q1", "diff_lambda_k1", "diff_lambda_q2",
          "diff_lambda_k2", "diff_subln_g", "swa_sinks", "w_in_c", "w_out_c", "rel_bias"]


def kernel(**inputs):
    import concourse.bacc as bacc
    import numpy as np
    from concourse.bass_utils import run_bass_kernel_spmd

    nc = bacc.Bacc("TRN2", target_bir_lowering=False, num_devices=1, dynamic_dma_scratch_size=1024)
    arrays, aps = {}, {}
    for name in INPUTS:
        a = np.ascontiguousarray(inputs[name])
        arrays[f"in_{name}"] = a
        aps[name] = nc.dram_tensor(f"in_{name}", a.shape, mybir.dt.from_np(a.dtype), kind="ExternalInput").ap()
    out = nc.dram_tensor("out_x", (1, SEQ, D), F32, kind="ExternalOutput").ap()
    build(nc, out=out, **aps)
    r = run_bass_kernel_spmd(nc, [arrays], core_ids=[0])
    return r.results[0]["out_x"]
```

```python
import math
from contextlib import ExitStack

import concourse.bass as bass
from concourse import mybir
from concourse.alu_op_type import AluOpType as ALU

F32 = mybir.dt.float32
F32R = mybir.dt.float32r
ACT = mybir.ActivationFunctionType

P = 128
SEQ = 1024
D = 1024
ST = SEQ // P
DT = D // P
HALF = 512
HD = 64
CHUNK = 64
A_HEADS, B_HEADS, C_HEADS = 4, 8, 16
REL_CLIP = 256
C_BAND_COLS = 5 * P
REL_ROW = 768
EPS = 1e-6
NEG = -1e30
HUGE = 3e38
LAM_INIT = 0.8 - 0.6 * math.exp(-0.3 * 0)
SCALE = HD ** -0.5


class Kind:

    def __init__(self, name, base, units, cols, slopes, shared_kv=False):
        self.name = name
        self.base = base
        self.units = units
        self.cols = cols
        self.slopes = slopes
        self.shared_kv = shared_kv
        self.groups = 8 if name == "A" else 16
        self.pvs = self.groups // 2

    def tiles(self, t):
        first = {"A": 0, "B": max(0, t - 1), "C": max(0, t - 4)}[self.name]
        return first, t + 1 - first

    def step(self, j):
        return (j % 2, j // 2) if self.name == "A" else (j // 8, j % 8)

    def slope(self, u, h):
        if not self.slopes:
            return 1.0
        head = u - self.base if self.name == "A" else 2 * (u - self.base) + h
        return 2.0 ** (-8 * (head + 1) // self.slopes)

    def group_of_step(self, j):
        if self.name == "A":
            return j // 2 if j % 2 else None
        return j

    def group(self, g):
        return (0, g) if self.name == "A" else (g // 8, g % 8)


KIND_A = Kind("A", 0, A_HEADS, dict(q=0, k=512, v=1024, g=2304), A_HEADS)
KIND_B = Kind("B", A_HEADS, B_HEADS // 2, dict(q=1536, k=2048, v=2176, g=2816), B_HEADS, True)
KIND_C = Kind("C", 0, C_HEADS // 2, dict(q=0, k=1024, v=2048, g=3072), None)


class Plan:

    def __init__(self, *kinds):
        self.kinds = kinds
        self.units = sum(k.units for k in kinds)
        self.loop = len(kinds) == 1

    def kind(self, u):
        return self.kinds[0] if self.loop else [k for k in self.kinds if k.base <= u][-1]

    def groups_before(self, u):
        if self.loop:
            return self.kinds[0].groups * u
        return sum(self.kind(v).groups for v in range(u))

    def pvs_before(self, u):
        if self.loop:
            return self.kinds[0].pvs * u
        return sum(self.kind(v).pvs for v in range(u))

    def nth(self, b, u):
        if b in "kv" and self.kind(u).shared_kv:
            return self.kind(u).base
        return u

    def projected(self, b, u):
        return u + 1 if b in "og" else self.nth(b, u)

    def loaded(self, b, u):
        return u + 1 if b == "o" else self.nth(b, u)

    def per_unit(self, u):
        return ["v"] if self.loop or self.nth("v", u + 1) == u + 1 else []

    def ahead(self, u):
        return ["k", "q"] if self.loop or self.nth("k", u + 1) == u + 1 else ["q"]


PLAN_AB = Plan(KIND_A, KIND_B)
PLAN_C = Plan(KIND_C)
STAGE_SLOT = dict(o=0, k=0, g=1, v=1, q=1)
PART_SLOT = dict(o=0, k=1, g=1, v=2, q=2)
FILLS = dict(o=16, g=2, v=2, q=2, k=2)
LAST_OUT_SLOT = 2
MMS = 48


def blocks_of(plan, u, first, last):
    blocks = [("g", u)]
    if not first:
        blocks.append(("o", u - 1))
    if not last:
        blocks += [(b, u + 1) for b in plan.per_unit(u) + plan.ahead(u)]
    return blocks


def blocks_before(plan, u, first):
    if first:
        return []
    if isinstance(u, int) and u == 1:
        return blocks_of(plan, 0, True, False)
    if isinstance(u, int) and not plan.loop:
        return blocks_before(plan, u - 1, False) + blocks_of(plan, u - 1, False, False)
    return blocks_of(plan, u - 1, False, False)


def previous_on(slot_map, before, blocks, n):
    for b, v in reversed(before + blocks[:n]):
        if slot_map[b] == slot_map[blocks[n][0]]:
            return b, v
    return None


def projections(blocks):
    return [(b, v) for b, v in blocks if b != "o"]


STEPS = 16
GATE_STEP = 1
TURN_LAG = 3
TAIL = TURN_LAG + 1


def slice_of(plan, u, last, s):
    n1 = MMS * (1 + (0 if last else len(plan.per_unit(u))))
    n2 = 0 if last else MMS * len(plan.ahead(u))
    if s < STEPS:
        return n1 * s // STEPS, n1 * (s + 1) // STEPS
    t = s - STEPS
    return n1 + n2 * t // TAIL, n1 + n2 * (t + 1) // TAIL


def done_fills(plan, u, first, last, s):
    lo, hi = slice_of(plan, u, last, s)
    out = []
    for n, (b, v) in enumerate(projections(blocks_of(plan, u, first, last))):
        for f in range(2):
            if lo < MMS * n + MMS // 2 * (f + 1) <= hi:
                out.append((b, v, f))
    return out


def out_fills(plan, first, s):
    start = GATE_STEP + 2
    if first or s < start:
        return range(0)
    span = STEPS + TAIL - start
    t = s - start
    return range(-(-FILLS["o"] * t // span), -(-FILLS["o"] * (t + 1) // span))


def ge(eng, sem, value):
    if isinstance(value, int) and value <= 0:
        return
    eng.wait_ge(sem, value)


def ge_apart(eng, passed, *waits):
    for sem, value in waits:
        ge(eng, sem, value)
    if not all(isinstance(value, int) for _, value in waits):
        eng.sem_inc(passed, 1)


def phase_semaphore(nc, env, name):
    s = nc.alloc_semaphore(name)
    env["phase_semaphores"].append(s)
    return s


def retire(nc, env):
    nc.clear_and_free_semaphores(env["phase_semaphores"])
    env["phase_semaphores"] = []
    nc.all_engine_barrier()


def mask(nc, tiles, name):
    n, width = tiles.shape[1], tiles.shape[2]
    late = tiles[:, :, width - CHUNK:width]
    last = nc.gpsimd.affine_select(out=late, in_=late, compare_op=ALU.is_ge, fill=NEG, base=-CHUNK,
                                   pattern=[[0, n], [0, CHUNK]], channel_multiplier=1)
    if name != "A":
        start = CHUNK if name == "B" else 0
        early = tiles[:, :, start:start + CHUNK]
        last = nc.gpsimd.affine_select(out=early, in_=early, compare_op=ALU.is_ge, fill=NEG, base=CHUNK - 1,
                                       pattern=[[0, n], [0, CHUNK]], channel_multiplier=-1)
    if name == "B":
        last = nc.gpsimd.memset(tiles[:, :, 0:CHUNK], NEG)
    return last


def alibi(nc, pool, tile, name, s_step, s_abs, s_bias):
    b, width = tile[:, 0, :], tile.shape[2]
    nc.gpsimd.iota(b, pattern=[[-1, width]], base=width - P, channel_multiplier=1,
                   allow_small_or_imprecise_dtypes=True).then_inc(s_step, 1)
    pool.wait_ge(s_abs, 1)
    nc.gpsimd.tensor_scalar(b, b, -1.0, 1.0, ALU.mult, ALU.mult).then_inc(s_step, 1)
    pool.wait_ge(s_step, 2)
    mask(nc, tile, name).then_inc(s_bias, 1)


def bias_tiles(env, name):
    if name == "A":
        return env["bias"][:, 0:SEQ].rearrange("p (a b) -> p a b", a=1)
    return env["bias"][:].rearrange("p (a b) -> p a b", a=2)


def boundary_phase(nc, n, env, x_src, x_dst, post_g, pre_g, plan=None, w_in=None, rel=None):
    y, hT_hi, hT_lo, ident = env["y"], env["hT_hi"], env["hT_lo"], env["ident"]
    w_f32, w_hi, w_lo, yT_hi, yT_lo = (env[k] for k in ("w_f32", "w_hi", "w_lo", "yT_hi", "yT_lo"))
    q_st, k_hh, k_l0, vT = (env[k] for k in ("q_st", "k_hh", "k_l0", "vT"))
    post, pre = post_g is not None, pre_g is not None
    lag = 3 if post else 0
    PAIR = 2 * P
    DVE_SUMS = range(ST) if pre else range(ST - 1, ST)
    with ExitStack() as ctx:
        def sb(name, shape, dt=F32):
            return ctx.enter_context(nc.sbuf_tensor(f"n{n}_{name}", shape, dt))

        def ps(name, shape):
            return ctx.enter_context(nc.psum_tensor(f"n{n}_{name}", shape, F32))

        def sem(name):
            return phase_semaphore(nc, env, f"n{n}_{name}")

        xb = sb("xb", [P, 3, D])
        xn = sb("xn", [P, 3, D])
        scaled = sb("scaled", [P, 2, D])
        junk = sb("junk", [P, D])
        g_post = sb("g_post", [P, D]) if post else None
        g_pre = sb("g_pre", [P, D]) if pre else None
        q_w = sb("q_w", [P, 2, D], F32R)
        stat = sb("stat", [P, 6, ST])
        eps, spare = sb("eps", [P, 1]), sb("spare", [P, 1])
        OUT_BANKS = 1 if pre else 4
        PROJ_BANKS = 3
        EARLY = 2 * (lag + 2) if pre else 0
        out_ps = ps("out_ps", [P, OUT_BANKS, HALF])
        tp = ps("tp", [P, 2, D]) if pre else None
        proj = ps("proj", [P, PROJ_BANKS, HALF]) if pre else None
        x_loaded, x_stored = [sem(f"x_loaded{i}") for i in range(3)], [sem(f"x_stored{i}") for i in range(3)]
        s_gpost, s_gpre, s_eps = sem("g_post_loaded"), sem("g_pre_loaded"), sem("eps_set")
        s_out, s_added, s_ysq, s_yroot, s_yrec, s_yscaled, s_xsum = (
            sem(k) for k in ("out_filled", "out_added", "ysq", "yroot", "yrec", "yscaled", "xsum"))
        s_xsq, s_xroot, s_xrec, s_xscaled, s_turned, s_hi, s_lo = (
            sem(k) for k in ("xsq", "xroot", "xrec", "xscaled", "turned", "hi_done", "lo_done"))
        w_loaded = {b: sem(f"w_loaded_{b}") for b in "vkqg"}
        w_hi_done = {b: sem(f"w_hi_done_{b}") for b in "vkqg"}
        w_ready = {b: sem(f"w_ready_{b}") for b in "vkqg"}
        filled = {b: sem(f"filled_{b}") for b in "kvq"}
        hi_out = {b: sem(f"hi_out_{b}") for b in "kq"}
        drained = {b: sem(f"drained_{b}") for b in "kvq"}
        s_ident, s_rel_in, s_rel_turned, s_zero = sem("ident"), sem("rel_loaded"), sem("rel_turned"), sem("zeroed")
        s_bstep, s_abs, s_bias = sem("bias_step"), sem("abs_done"), sem("bias_ready")
        if rel:
            table = sb("rel_in", [C_HEADS, 2 * REL_CLIP + 1])
            rows = sb("rel_rows", [C_HEADS, REL_ROW])
            rel_width = C_BAND_COLS - REL_CLIP - 1
        stage = dict(v=1, k=0, q=1, g=0)
        parts = dict(v=(w_hi[:, 0, :], w_lo[:, 0, :]), k=(w_hi[:, 1, :], w_lo[:, 1, :]), q=(q_w[:, 0, :], q_w[:, 1, :]),
                     g=(w_hi[:, 1, :], w_lo[:, 1, :]))
        block = ctx.enter_context(nc.Block())

        def x_tile(i):
            return xn[:, i % 3, :] if post else xb[:, i % 3, :]

        def out_bank(f):
            if f < EARLY and f % (PROJ_BANKS + 1):
                return proj[:, f % (PROJ_BANKS + 1) - 1, :]
            return out_ps[:, 0 if f < EARLY else f % OUT_BANKS, :]

        def pair_blocks(i):
            t = i - lag - 2
            if not pre or not 0 <= t < ST:
                return []
            return [("q", t // 2)] if t % 2 else [("k", t // 2), ("v", t // 2)]

        SEQUENCE = [bp for i in range(ST + lag + 2) for bp in pair_blocks(i)]

        @block.sync
        def _(sp):
            def load_x(i):
                if i >= 3:
                    sp.wait_ge(s_xsum if post else s_xscaled, i - 2)
                    if not post:
                        sp.wait_ge(s_xsq, i - 2)
                sp.dma_start(xb[:, i % 3, :], x_src[i * P:(i + 1) * P, :]).then_inc(x_loaded[i % 3], 16)

            def load_w(b, after):
                if after:
                    sp.wait_ge(w_ready[after], 1)
                c0 = plan.kind(0).cols[b]
                sp.dma_start(w_f32[:, stage[b], :].rearrange("p (t n) -> p t n", t=DT),
                             w_in.rearrange("(t p) n -> p t n", p=P)[:, :, c0:c0 + P]).then_inc(w_loaded[b], 16)

            if post:
                sp.dma_start(g_post[:], post_g.partition_broadcast(P)).then_inc(s_gpost, 16)
            load_x(0)
            if pre:
                sp.dma_start(g_pre[:], pre_g.partition_broadcast(P)).then_inc(s_gpre, 16)
            load_x(1)
            if pre:
                load_w("k", None)
                load_w("v", None)
            load_x(2)
            if rel:
                sp.dma_start(table[:], rel["table"]).then_inc(s_rel_in, 16)
            for i in range(3, ST + 3):
                if i < ST:
                    load_x(i)
                if post and i - 3 < ST:
                    sp.wait_ge(s_xsum, i - 2)
                    sp.dma_start(x_dst[(i - 3) * P:(i - 2) * P, :], xn[:, (i - 3) % 3, :]).then_inc(x_stored[i % 3], 16)
                if pre and i == 3:
                    load_w("q", "v")
                    load_w("g", "k")
                if rel and i == 6:
                    sp.wait_ge(s_rel_turned, 2)
                    sp.dma_start(rel["rows"].ap(), rows[:]).then_inc(rel["stored"], 16)
            if rel:
                sp.wait_ge(rel["stored"], 16)
                sp.dma_start(rel["tiles"].ap().rearrange("p h c -> h p c"),
                             bass.AP(rel["rows"], P - 1, [[REL_ROW, C_HEADS], [-1, P], [1, C_BAND_COLS]]))\
                    .then_inc(rel["stored"], 16)
            if post:
                for slot in range(3):
                    sp.wait_ge(x_stored[slot], 16 * ((ST - 1 - slot) // 3 + 1))

        @block.gpsimd
        def _(pool):
            def split(b):
                hi, lo = parts[b]
                src = w_f32[:, stage[b], :]
                pool.wait_ge(w_loaded[b], 16)
                nc.gpsimd.tensor_scalar(hi, src, 1.0, 1.0, ALU.mult, ALU.mult).then_inc(w_hi_done[b], 1)
                pool.wait_ge(w_hi_done[b], 1)
                nc.gpsimd.tensor_tensor(lo, src, hi, ALU.subtract).then_inc(w_ready[b], 1)

            nc.gpsimd.memset(eps[:], EPS).then_inc(s_eps, 1)
            if rel:
                nc.gpsimd.memset(ident[:], 0.0).then_inc(s_ident, 1)
                pool.wait_ge(s_ident, 1)
                nc.gpsimd.affine_select(out=ident[:], in_=ident[:], compare_op=ALU.not_equal, fill=1.0, base=0,
                                        pattern=[[-1, P]], channel_multiplier=1).then_inc(s_ident, 1)
            if pre:
                split("k")
                split("v")
            if pre and post:
                split("q")
            if not post:
                nc.gpsimd.memset(k_l0[:].bitcast(F32), 0.0).then_inc(s_zero, 1)
                split("q")
                alibi(nc, pool, bias_tiles(env, "A"), "A", s_bstep, s_abs, s_bias)
                nc.gpsimd.memset(y[:], 0.0)
            for i in range(ST if post else 0):
                pool.wait_ge(s_yscaled, i + 1)
                if i not in DVE_SUMS:
                    pool.wait_ge(x_loaded[i % 3], 16 * (i // 3 + 1))
                    nc.gpsimd.tensor_tensor(xn[:, i % 3, :], xn[:, i % 3, :], xb[:, i % 3, :], ALU.add)\
                        .then_inc(s_xsum, 1)
                if pre:
                    nc.gpsimd.memset(y[:, i, :], 0.0)
            if pre:
                pool.wait_ge(filled["k"], ST // 2)
                split("g")

        @block.scalar
        def _(act):
            copy = nc.scalar.activation

            def root(src_sem, col, i, done):
                act.wait_ge(src_sem, i + 1)
                copy(stat[:, col + 1, i:i + 1], stat[:, col, i:i + 1], ACT.Sqrt, scale=1.0 / D, bias=eps[:]).then_inc(done, 1)

            act.wait_ge(s_eps, 1)
            copy(spare[:], eps[:], ACT.Sqrt)
            for i in range(ST + lag + 3):
                j = i - lag
                if pre and 0 <= j < ST:
                    if post:
                        act.wait_ge(s_xsum, j + 1)
                    else:
                        act.wait_ge(x_loaded[j % 3], 16 * (j // 3 + 1))
                    copy(junk[:], x_tile(j), ACT.Square, accum_out=stat[:, 3, j:j + 1]).then_inc(s_xsq, 1)
                    root(s_xsq, 3, j, s_xroot)
                j = i - lag - 1
                if pre and 0 <= j < ST:
                    act.wait_ge(s_turned, j + 1)
                    copy(hT_hi[:, :, j * P:(j + 1) * P], tp[:, j % 2, :].rearrange("p (d s) -> p d s", d=DT),
                         ACT.Copy).then_inc(s_hi, 1)
                if post and i < ST:
                    act.wait_ge(s_added, 2 * i + 2)
                    copy(junk[:], y[:, i, :], ACT.Square, accum_out=stat[:, 0, i:i + 1]).then_inc(s_ysq, 1)
                    root(s_ysq, 0, i, s_yroot)
                if i == 6 and not post:
                    act.wait_ge(s_bstep, 1)
                    copy(bias_tiles(env, "A"), bias_tiles(env, "A"), ACT.Abs).then_inc(s_abs, 1)
                for b, pair in pair_blocks(i - 1):
                    act.wait_ge(filled[b], pair + 1)
                    bank = proj[:, SEQUENCE.index((b, pair)) % PROJ_BANKS, 0:PAIR]
                    cols = slice(pair * PAIR, (pair + 1) * PAIR)
                    if b == "v":
                        copy(vT[:, cols], bank, ACT.Copy).then_inc(drained[b], 1)
                    for h in range(2) if b != "v" else ():
                        head = bank[h * HD:(h + 1) * HD, :]
                        if b == "q":
                            last = copy(q_st[0:HD, h, cols], head, ACT.Copy, scale=SCALE / plan.kind(0).slope(0, h))
                        else:
                            copy(k_hh[0:HD, h, cols], head, ACT.Copy)
                            last = copy(k_hh[HD:P, h, cols], head, ACT.Copy)
                    if b != "v":
                        last.then_inc(hi_out[b], 1)

        @block.vector
        def _(dve):
            tt, stt = nc.vector.tensor_tensor, nc.vector.scalar_tensor_tensor

            def reciprocal(col, i, after, done):
                dve.wait_ge(after, i + 1)
                nc.vector.reciprocal(stat[:, col + 2, i:i + 1], stat[:, col + 1, i:i + 1]).then_inc(done, 1)
                dve.wait_ge(done, i + 1)

            def add_out(f):
                dve.wait_ge(s_out, f + 1)
                into = y[:, f // 2, (f % 2) * HALF:(f % 2 + 1) * HALF]
                tt(into, out_bank(f), into, ALU.add).then_inc(s_added, 1)

            for i in range(ST + lag + 3):
                j = i - lag
                if pre and 0 <= j < ST:
                    reciprocal(3, j, s_xroot, s_xrec)
                    if j == 0:
                        dve.wait_ge(s_gpre, 16)
                    if j >= 2:
                        dve.wait_ge(s_turned, j - 1)
                    stt(out=scaled[:, j % 2, :], in0=x_tile(j), scalar=stat[:, 5, j:j + 1], in1=g_pre[:], op0=ALU.mult,
                        op1=ALU.mult).then_inc(s_xscaled, 1)
                j = i - lag - 1
                if pre and 0 <= j < ST:
                    dve.wait_ge(s_hi, j + 1)
                    tt(hT_lo[:, :, j * P:(j + 1) * P], tp[:, j % 2, :].rearrange("p (d s) -> p d s", d=DT),
                       hT_hi[:, :, j * P:(j + 1) * P], ALU.subtract).then_inc(s_lo, 1)
                if post and i < ST:
                    add_out(2 * i)
                if post and i < ST:
                    add_out(2 * i + 1)
                j = i - 1
                if post and 0 <= j < ST:
                    reciprocal(0, j, s_yroot, s_yrec)
                    if j == 0:
                        dve.wait_ge(s_gpost, 16)
                    if j >= 3:
                        dve.wait_ge(x_stored[j % 3], 16 * (j // 3))
                        if pre:
                            dve.wait_ge(s_xscaled, j - 2)
                            dve.wait_ge(s_xsq, j - 2)
                    stt(out=xn[:, j % 3, :], in0=y[:, j, :], scalar=stat[:, 2, j:j + 1], in1=g_post[:], op0=ALU.mult,
                        op1=ALU.mult).then_inc(s_yscaled, 1)
                    if j in DVE_SUMS:
                        dve.wait_ge(s_yscaled, j + 1)
                        dve.wait_ge(x_loaded[j % 3], 16 * (j // 3 + 1))
                        ge(dve, s_xsum, j)
                        tt(xn[:, j % 3, :], xn[:, j % 3, :], xb[:, j % 3, :], ALU.add).then_inc(s_xsum, 1)
                for b, pair in pair_blocks(i - 1):
                    if b == "v":
                        continue
                    dve.wait_ge(hi_out[b], pair + 1)
                    bank = proj[:, SEQUENCE.index((b, pair)) % PROJ_BANKS, 0:PAIR]
                    cols = slice(pair * PAIR, (pair + 1) * PAIR)
                    if b == "k" and pair == 0 and not post:
                        dve.wait_ge(s_zero, 1)
                    for h in range(2):
                        head = bank[h * HD:(h + 1) * HD, :]
                        if b == "q":
                            last = stt(out=q_st[HD:P, h, cols], in0=head, scalar=SCALE / plan.kind(0).slope(0, h),
                                       in1=q_st[0:HD, h, cols], op0=ALU.mult, op1=ALU.subtract)
                        else:
                            last = tt(k_l0[0:HD, h, cols], head, k_hh[0:HD, h, cols], ALU.subtract)
                    last.then_inc(drained[b], 1)
                if rel and i == 3:
                    dve.wait_ge(s_rel_in, 16)
                    nc.vector.tensor_copy(rows[:, 0:rel_width], table[:, 2 * REL_CLIP:2 * REL_CLIP + 1]
                                          .broadcast_to([C_HEADS, rel_width])).then_inc(s_rel_turned, 1)
                    nc.vector.tensor_copy(rows[:, rel_width:REL_ROW],
                                          table[:, 2 * REL_CLIP + 1 - (REL_ROW - rel_width):][:, ::-1])\
                        .then_inc(s_rel_turned, 1)

        @block.tensor
        def _(pe):
            mm = nc.tensor.matmul

            def project_out(f):
                ge(pe, s_added, f - PROJ_BANKS if f < EARLY else f - OUT_BANKS + 1)
                rows_of, cols = slice(f // 2 * P, (f // 2 + 1) * P), slice((f % 2) * HALF, (f % 2 + 1) * HALF)
                w, w_l = w_hi[:, LAST_OUT_SLOT, cols], w_lo[:, LAST_OUT_SLOT, cols]
                for m, (lhs, rhs) in enumerate(((yT_hi, w), (yT_hi, w_l), (yT_lo, w))):
                    last = mm(out_bank(f), lhs[:, rows_of], rhs, start=m == 0, stop=m == 2)
                last.then_inc(s_out, 1)

            if rel:
                pe.wait_ge(s_ident, 2)
            for i in range(ST + lag + 2):
                if post and i < ST:
                    project_out(2 * i)
                if post and i < ST and 2 * i + 1 < EARLY:
                    project_out(2 * i + 1)
                j = i - lag
                if pre and 0 <= j < ST:
                    pe.wait_ge(s_xscaled, j + 1)
                    if j >= 2:
                        pe.wait_ge(s_lo, j - 1)
                    for d in range(DT):
                        last = nc.tensor.transpose(tp[:, j % 2, d * P:(d + 1) * P], scaled[:, j % 2, d * P:(d + 1) * P],
                                                   ident[:])
                    last.then_inc(s_turned, 1)
                if post and i < ST and 2 * i + 1 >= EARLY:
                    project_out(2 * i + 1)
                for b, pair in pair_blocks(i):
                    f = SEQUENCE.index((b, pair))
                    if pair == 0:
                        pe.wait_ge(w_ready[b], 1)
                    pe.wait_ge(s_lo, 2 * pair + 2)
                    if f >= PROJ_BANKS:
                        before, its_pair = SEQUENCE[f - PROJ_BANKS]
                        pe.wait_ge(drained[before], its_pair + 1)
                    cols = slice(pair * PAIR, (pair + 1) * PAIR)
                    hi, lo = parts[b]
                    for d in range(DT):
                        for m, (lhs, rhs) in enumerate(((hi, hT_hi), (hi, hT_lo), (lo, hT_hi))):
                            last = mm(proj[:, f % PROJ_BANKS, 0:PAIR], lhs[:, d * P:(d + 1) * P], rhs[:, d, cols],
                                      start=d == 0 and m == 0, stop=d == DT - 1 and m == 2)
                    last.then_inc(filled[b], 1)


def mixer_phase(nc, plan, env, w_in, w_out, small, rel_tiles=None):
    y, hT_hi, hT_lo, ident = env["y"], env["hT_hi"], env["hT_lo"], env["ident"]
    U, NS, LOOP = plan.units, STEPS, plan.loop
    PHASE = "".join(k.name for k in plan.kinds)
    AB = not LOOP
    BW = SEQ if AB else C_BAND_COLS
    BW_B = 2 * P
    R0 = 0 if AB else 2
    w_view = w_in.rearrange("(t p) n -> p t n", p=P)
    groups_before, pvs_before, nth = plan.groups_before, plan.pvs_before, plan.nth
    with ExitStack() as ctx:
        def sb(name, shape, dt=F32):
            return ctx.enter_context(nc.sbuf_tensor(f"{PHASE}_{name}", shape, dt))

        def ps(name, shape):
            return ctx.enter_context(nc.psum_tensor(f"{PHASE}_{name}", shape, F32))

        def sem(name):
            return phase_semaphore(nc, env, f"{PHASE}_{name}")

        w_f32, w_hi, w_lo, yT_hi, yT_lo = (env[k] for k in ("w_f32", "w_hi", "w_lo", "yT_hi", "yT_lo"))
        q_st, k_hh, k_l0, vT = (env[k] for k in ("q_st", "k_hh", "k_l0", "vT"))
        v_st = sb("v_st", [P, 2, ST, P], F32R)
        gate = sb("gate", [P, SEQ])
        o_sb = sb("o_sb", [P, SEQ])
        pT_hi = sb("pT_hi", [P, 8 - R0, 2 * P], F32R)
        pT_lo = sb("pT_lo", [P, 8 - R0, 2 * P], F32R)
        e_sb = sb("e_sb", [P, 4, BW])
        bias = bias_tiles(env, "A" if AB else "C")
        stats = sb("stats", [P, 5, 16])
        low, total, rec, sink_e, den = (stats[:, i, :] for i in range(5))
        dense = ps("dense", [P, 3, HALF])
        scores = ps("scores", [P, SEQ])
        turned = ps("turned", [P, SEQ])
        pv_ps = ps("pv_ps", [P, 2, 2 * P])

        w_loaded = {b: sem(f"w_loaded_{b}") for b in FILLS}
        w_hi_done = {b: sem(f"w_hi_done_{b}") for b in FILLS}
        w_ready = {b: sem(f"w_ready_{b}") for b in FILLS}
        filled = {b: sem(f"filled_{b}") for b in FILLS}
        hi_out = {b: sem(f"hi_out_{b}") for b in FILLS if b != "o"}
        drained = {b: sem(f"drained_{b}") for b in FILLS}
        s_scores, s_low, s_exp, s_rec, s_probs = (sem(n) for n in ("scored", "low_done", "exp_done", "rec_done", "probs"))
        s_turn, s_phi, s_plo, s_pv, s_pvc, s_out = (sem(n) for n in
                                                    ("turned_g", "p_hi", "p_lo", "pv_done", "pv_low", "out_part"))
        s_vturn, s_vhi, s_vlo, s_y, s_yhi, s_ylo = (sem(n) for n in
                                                    ("v_turned", "v_hi", "v_lo", "y_done", "y_hi", "y_lo"))
        s_zero, s_bias, s_const, s_passed = sem("zeroed"), sem("bias_ready"), sem("const_ready"), sem("passed")
        if AB:
            ones, rms = sb("ones", [P, 1]), sb("rms", [P, 2, ST])
            neg_lam, g_sub, eps = sb("neg_lam", [P, 1]), sb("g_sub", [P, 1]), sb("eps", [P, 1])
            lam_in, lam_prod, lam_sum = sb("lam_in", [P, 4, HD]), sb("lam_prod", [P, HD]), sb("lam_sum", [P, 4])
            bias_b, sinks = sb("bias_b", [P, 1, BW_B])[:], sb("sinks", [P, 2, B_HEADS])
            s_abs, s_bstep, s_mid, s_den = sem("abs_done"), sem("bias_step"), sem("mid_done"), sem("den_done")
            s_sq, s_ssum, s_root, s_rroot, s_lam = (sem(n) for n in ("squared", "sq_summed", "root", "rroot", "lam_step"))
            s_sink, s_negsink = sem("sink_e"), sem("neg_sink")
        B_UNSEEN = 5
        ZEROED = 4 if AB else 2

        def run_units(eng, unit):
            unit(0, True, False)
            if LOOP:
                unit(1, False, False)
                with eng.Fori(2, U - 1) as u:
                    unit(u, False, False)
            else:
                for u in range(1, U - 1):
                    unit(u, False, False)
            unit(U - 1, False, True)

        def transposed_after(u, s):
            j = s - TURN_LAG
            return plan.kind(u).group_of_step(j) if 0 <= j < NS else None

        def pv_in(u, s):
            g = transposed_after(u, s - 1) if s >= 1 else None
            return g // 2 if g is not None and g % 2 else None

        def v_head(u, h):
            return (u - plan.kind(u).base) // 2 if plan.kind(u).name == "B" else h

        def score_bank(kind, j):
            return j % 2 if kind.name == "B" else 0

        def turned_bank(kind, g):
            return g % 2 if kind.name == "B" else 0

        def turned_group(kind, g, n):
            at = turned_bank(kind, g) * HALF
            return turned[:, at:at + n * P].rearrange("p (n q) -> p n q", n=n)

        def e_of(j):
            return j % 4

        block = ctx.enter_context(nc.Block())

        @block.sync
        def _(sp):
            def settled(offset):
                return offset if isinstance(offset, int) else sp.snap(offset)

            def source(b, u):
                if b == "o":
                    return w_out[bass.ds(settled(u * P), P), :]
                kind = plan.kind(u)
                c0 = kind.cols[b] + (u - kind.base) * P
                return w_view[:, :, bass.ds(settled(c0), P)]

            def load(b, src):
                slot = w_f32[:, STAGE_SLOT[b], :]
                sp.dma_start(slot if b == "o" else slot.rearrange("p (t n) -> p t n", t=DT), src)\
                    .then_inc(w_loaded[b], 16)

            def load_all(u, first, last):
                blocks, before = blocks_of(plan, u, first, last), blocks_before(plan, u, first)
                sources = [source(b, v) for b, v in blocks]
                for n, (b, v) in enumerate(blocks):
                    if first and b == "g":
                        continue
                    prev = previous_on(STAGE_SLOT, before, blocks, n)
                    if prev:
                        ge_apart(sp, s_passed, (w_ready[prev[0]], plan.loaded(*prev)))
                    load(b, sources[n])

            def load_bias(u, wait):
                if wait:
                    sp.wait_ge(s_low, NS * u)
                sp.dma_start(bias, rel_tiles.ap()[:, bass.ds(2 * u, 2), :]).then_inc(s_const, 16)

            if AB:
                for i, name in enumerate(("q1", "k1", "q2", "k2")):
                    sp.dma_start(lam_in[:, i, :], small[name].partition_broadcast(P)).then_inc(s_const, 16)
                sp.dma_start(g_sub[:], small["g"].rearrange("(p a) -> p a", a=1)).then_inc(s_const, 16)
                sp.dma_start(sinks[:, 0, :], small["sinks"].partition_broadcast(P)).then_inc(s_const, 16)
            if LOOP:
                sp.wait_ge(env["rel_stored"], 32)
                load_bias(0, False)

            def unit(u, first, last):
                if LOOP and not first:
                    load_bias(u, True)
                load_all(u, first, last)
            run_units(sp, unit)
            sp.wait_ge(w_ready["o"], U - 1)
            load("o", source("o", U - 1))

        @block.gpsimd
        def _(pool):
            ts = nc.gpsimd.tensor_scalar

            def split(b, u, prev, slot=None):
                slot = PART_SLOT[b] if slot is None else slot
                ge_apart(pool, s_passed, (w_loaded[b], 16 * plan.loaded(b, u)),
                         *([(filled[prev[0]], FILLS[prev[0]] * plan.projected(*prev))] if prev else []))
                src, hi = w_f32[:, STAGE_SLOT[b], :], w_hi[:, slot, :]
                ts(hi, src, 1.0, 1.0, ALU.mult, ALU.mult).then_inc(w_hi_done[b], 1)
                pool.wait_ge(w_hi_done[b], plan.loaded(b, u))
                nc.gpsimd.tensor_tensor(w_lo[:, slot, :], src, hi, ALU.subtract).then_inc(w_ready[b], 1)

            if AB:
                nc.gpsimd.memset(ones[:], 1.0).then_inc(s_zero, 1)
                nc.gpsimd.memset(eps[:], EPS).then_inc(s_zero, 1)
            nc.gpsimd.memset(pT_hi[:].bitcast(F32), 0.0).then_inc(s_zero, 1)
            nc.gpsimd.memset(pT_lo[:].bitcast(F32), 0.0).then_inc(s_zero, 1)
            if AB:
                alibi(nc, pool, bias_b, "B", s_bstep, s_abs, s_bias)

            def unit(u, first, last):
                blocks, before = blocks_of(plan, u, first, last), blocks_before(plan, u, first)
                if not first:
                    split(*blocks[0], previous_on(PART_SLOT, before, blocks, 0))
                if LOOP:
                    ge_apart(pool, s_passed, (s_const, 16 * (u + 1)))
                    mask(nc, bias, "C").then_inc(s_bias, 1)
                if AB and u == KIND_B.base:
                    pool.wait_ge(s_pv, pvs_before(u))
                    for p_part in (pT_hi, pT_lo):
                        nc.gpsimd.memset(p_part[:, B_UNSEEN, P:2 * P].bitcast(F32), 0.0).then_inc(s_zero, 1)
                for n in range(1, len(blocks)):
                    split(*blocks[n], previous_on(PART_SLOT, before, blocks, n))
            run_units(pool, unit)
            split("o", U - 1, ("q", U - 1), LAST_OUT_SLOT)

        @block.tensor
        def _(pe):
            mm = nc.tensor.matmul

            def project(blocks, last_before, lo, hi):
                for m in range(lo, hi):
                    n, i = m // MMS, m % MMS
                    b, u = blocks[n]
                    f, d, part = i // (MMS // 2), i % (MMS // 2) // 3, i % 3
                    w, w_l = w_hi[:, PART_SLOT[b], :], w_lo[:, PART_SLOT[b], :]
                    if i == 0:
                        ge(pe, w_ready[b], plan.loaded(b, u))
                    if i % (MMS // 2) == 0:
                        pb, pu = blocks[n - 1] if n else last_before if last_before else (None, 0)
                        if pb:
                            ge(pe, drained[pb], 2 * plan.projected(pb, pu) + f - 1)
                    lhs, rhs = ((w, hT_hi), (w, hT_lo), (w_l, hT_hi))[part]
                    last = mm(dense[:, f, :], lhs[:, d * P:(d + 1) * P], rhs[:, d, f * HALF:(f + 1) * HALF],
                              start=d == 0 and part == 0, stop=d == DT - 1 and part == 2)
                    if d == DT - 1 and part == 2:
                        last.then_inc(filled[b], 1)

            def project_out(u, f):
                s, half = f // 2, f % 2
                if f == 0:
                    ge(pe, w_ready["o"], u + 1)
                    ge(pe, s_ylo, u + 1)
                    if plan.kind(u).name == "A":
                        ge(pe, s_root, u + 1)
                ge(pe, drained["o"], FILLS["o"] * u + f)
                w, w_l = w_hi[:, PART_SLOT["o"], :], w_lo[:, PART_SLOT["o"], :]
                for n, (lhs, rhs) in enumerate(((yT_hi, w), (yT_hi, w_l), (yT_lo, w))):
                    last = mm(dense[:, 2, :], lhs[:, s * P:(s + 1) * P], rhs[:, half * HALF:(half + 1) * HALF],
                              start=n == 0, stop=n == 2)
                last.then_inc(filled["o"], 1)

            def turn_v(u):
                for s in range(ST):
                    last = nc.tensor.transpose(turned[:, s * P:(s + 1) * P], vT[:, s * P:(s + 1) * P], ident[:])
                last.then_inc(s_vturn, 1)

            def score(u, j):
                kind = plan.kind(u)
                h, t = kind.step(j)
                kh = v_head(u, h)
                k0, n = kind.tiles(t)
                n1 = n * P if n <= 4 else {5: 256, 6: 384, 7: 384, 8: 512}[n]
                off = HALF - n1 if n > 4 else score_bank(kind, j) * HALF
                if j == 0:
                    ge(pe, drained["q"], 2 * plan.projected("q", u))
                    ge(pe, drained["k"], 2 * plan.projected("k", u))
                ge(pe, s_low, NS * u + j - (kind.name == "B" and j > 0))
                parts = [(off, k0 * P, n1)] + ([(HALF, k0 * P + n1, n * P - n1)] if n > 4 else [])
                for at, key, w in parts:
                    for i, k_part in enumerate((k_hh, k_l0)):
                        last = mm(scores[:, at:at + w], q_st[:, h, t * P:(t + 1) * P], k_part[:, kh, key:key + w],
                                  start=i == 0, stop=i == 1)
                last.then_inc(s_scores, 1)

            def turn(u, g):
                kind = plan.kind(u)
                h, t = kind.group(g)
                e = e_of(2 * g) if kind.name == "A" else e_of(g)
                n, at = kind.tiles(t)[1], turned_bank(kind, g) * HALF
                ge(pe, s_probs, groups_before(u) + g + 1)
                if g == 0:
                    ge(pe, s_vlo, nth("v", u) + 1)
                ge(pe, s_plo, groups_before(u) + g - (kind.name == "B" and g > 0))
                for i in range(n):
                    last = nc.tensor.transpose(turned[:, at + i * P:at + (i + 1) * P], e_sb[:, e, i * P:(i + 1) * P],
                                               ident[:])
                last.then_inc(s_turn, 1)

            def times_v(u, n):
                kind = plan.kind(u)
                h, t = kind.group(2 * n)
                vh = v_head(u, h)
                k0 = kind.tiles(t)[0]
                count = t + 2 - k0
                ge(pe, s_plo, groups_before(u) + 2 * n + 2)
                ge(pe, s_out, pvs_before(u) + n - 1)
                if n == 0 and isinstance(u, int) and u == 0:
                    pe.wait_ge(s_zero, ZEROED)
                if n == 0 and AB and u == KIND_B.base:
                    pe.wait_ge(s_zero, ZEROED + 2)
                out = pv_ps[:, n % 2, :]
                if kind.name == "A":
                    parts = ((0, pT_hi), (0, pT_lo), (1, pT_hi))
                else:
                    parts = ((vh, pT_hi), (vh, pT_lo))
                for i in range(count):
                    kt = k0 + i
                    r = kt - t + 6 - R0
                    for x, (which, p_part) in enumerate(parts):
                        last = mm(out, v_st[:, which, kt, :], p_part[:, r, :], start=i == 0 and x == 0,
                                  stop=i == count - 1 and x == len(parts) - 1)
                last.then_inc(s_pv, 1)

            def square_sums(u):
                ge(pe, s_sq, u + 1)
                ge(pe, drained["o"], FILLS["o"] * u)
                for t in range(ST):
                    last = mm(dense[:, 2, t:t + 1], vT[:, t * P:(t + 1) * P], ones[:], start=True, stop=True)
                last.then_inc(s_ssum, 1)

            turn_v(0)

            def unit(u, first, last):
                blocks = projections(blocks_of(plan, u, first, last))
                before = None if first else projections(blocks_before(plan, u, first))[-1]
                for s in range(NS + TAIL):
                    lo, hi = slice_of(plan, u, last, s)
                    fills = out_fills(plan, first, s)
                    if len(fills) > 1:
                        project_out(u - 1, fills[0])
                    project(blocks, before, lo, hi)
                    if AB and s == 1 and 0 < u <= A_HEADS:
                        square_sums(u - 1)
                    if len(fills) > 0:
                        project_out(u - 1, fills[-1])
                    if pv_in(u, s) is not None:
                        times_v(u, pv_in(u, s))
                    if transposed_after(u, s) is not None:
                        turn(u, transposed_after(u, s))
                    if s < NS:
                        score(u, s)
                if not last and plan.per_unit(u):
                    ge(pe, drained["v"], 2 * plan.projected("v", u + 1))
                    ge(pe, s_plo, groups_before(u + 1))
                    turn_v(u + 1)
            run_units(pe, unit)

        @block.scalar
        def _(act):
            copy = nc.scalar.activation

            def hi_of_fill(b, u, f):
                act.wait_ge(filled[b], 2 * plan.projected(b, u) + f - 1)
                bank, cols = dense[:, f, :], slice(f * HALF, (f + 1) * HALF)
                if b == "g":
                    if not (isinstance(u, int) and u == 0):
                        act.wait_ge(s_y, u)
                    copy(gate[:, cols], bank, ACT.Tanh, scale=0.5).then_inc(hi_out[b], 1)
                if b == "v":
                    if not (isinstance(u, int) and u == 0):
                        act.wait_ge(s_vturn, u)
                    copy(vT[:, cols], bank, ACT.Copy).then_inc(drained[b], 1)
                if b == "q":
                    for h in range(2):
                        last = copy(q_st[0:HD, h, cols], bank[h * HD:(h + 1) * HD, :], ACT.Copy,
                                    scale=SCALE / plan.kind(u).slope(u, h))
                    last.then_inc(hi_out[b], 1)
                if b == "k":
                    for h in range(2):
                        for half in range(2):
                            last = copy(k_hh[half * HD:(half + 1) * HD, h, cols], bank[h * HD:(h + 1) * HD, :], ACT.Copy)
                    last.then_inc(hi_out[b], 1)

            def exp(u, j):
                kind = plan.kind(u)
                h, t = kind.step(j)
                n = kind.tiles(t)[1] * P
                e = e_sb[:, e_of(j), 0:n]
                ge(act, s_low, NS * u + j + 1)
                copy(e, e, ACT.Exp, scale=-1.0, bias=low[:, j:j + 1], accum_out=total[:, j:j + 1]).then_inc(s_exp, 1)
                if kind.name == "B":
                    head = 2 * (u - kind.base) + h
                    copy(sink_e[:, j:j + 1], low[:, j:j + 1], ACT.Exp, bias=sinks[:, 0, head:head + 1]).then_inc(s_sink, 1)

            def hi_of_group(u, g):
                kind = plan.kind(u)
                h, t = kind.group(g)
                k0, n = kind.tiles(t)
                r = k0 - (t - t % 2) + 6 - R0
                ge(act, s_turn, groups_before(u) + g + 1)
                if g == 0 and isinstance(u, int) and u == 0:
                    act.wait_ge(s_zero, ZEROED)
                if g % 2 == 0:
                    ge(act, s_pv, pvs_before(u) + g // 2)
                copy(pT_hi[:, r:r + n, (t % 2) * P:(t % 2 + 1) * P],
                     turned_group(kind, g, n), ACT.Copy).then_inc(s_phi, 1)

            def out_low(u, n):
                kind = plan.kind(u)
                h, t = kind.group(2 * n)
                ge(act, s_pv, pvs_before(u) + n + 1)
                if n == 0:
                    ge(act, s_ylo, u)
                cols = slice(t * P, (t + 2) * P)
                if kind.name == "A":
                    copy(o_sb[:, cols], pv_ps[:, n % 2, :], ACT.Copy).then_inc(s_out, 1)
                else:
                    copy(o_sb[h * HD:(h + 1) * HD, cols], pv_ps[HD:P, n % 2, :], ACT.Copy).then_inc(s_pvc, 1)

            def hi_of_v(u):
                ge(act, s_vturn, nth("v", u) + 1)
                if plan.kind(u).name == "A":
                    copy(v_st[:, 0, :, :], turned[:].rearrange("p (s f) -> p s f", s=ST), ACT.Copy).then_inc(s_vhi, 1)
                else:
                    copy(v_st[:, :, :, 0:HD], turned[:].rearrange("p (s h f) -> p h s f", s=ST, h=2), ACT.Copy)\
                        .then_inc(s_vhi, 1)

            hi_of_v(0)

            def hi_of_gated(u):
                ge(act, s_y, u + 1)
                ge(act, filled["o"], FILLS["o"] * u)
                copy(yT_hi[:], o_sb[:], ACT.Copy).then_inc(s_yhi, 1)

            def root_mean(u):
                act.wait_ge(s_ssum, u + 1)
                ge(act, drained["o"], FILLS["o"] * u)
                copy(rms[:, 0, :], dense[:, 2, 0:ST], ACT.Sqrt, scale=1.0 / P, bias=eps[:]).then_inc(s_root, 1)

            def unit(u, first, last):
                for s in range(NS + TAIL):
                    g = transposed_after(u, s - 1) if s >= 1 else None
                    if g is not None:
                        hi_of_group(u, g)
                    if 1 <= s <= NS:
                        exp(u, s - 1)
                    for b, v, f in done_fills(plan, u, first, last, s):
                        hi_of_fill(b, v, f)
                    if pv_in(u, s) is not None:
                        out_low(u, pv_in(u, s))
                    if AB and s == 1 and 0 < u <= A_HEADS:
                        root_mean(u - 1)
                    if s == GATE_STEP and not first:
                        hi_of_gated(u - 1)
                    if s == 1 and AB and first:
                        act.wait_ge(s_lam, 2)
                        copy(lam_sum[:, 2:4], lam_sum[:, 0:2], ACT.Exp).then_inc(s_lam, 1)
                    if s == 2 and AB and first:
                        act.wait_ge(s_bstep, 1)
                        copy(bias_b, bias_b, ACT.Abs).then_inc(s_abs, 1)
                if not last and plan.per_unit(u):
                    hi_of_v(u + 1)
                if plan.kind(u).name == "A":
                    ge(act, s_out, pvs_before(u + 1))
                    copy(vT[:], o_sb[:], ACT.Square).then_inc(s_sq, 1)
            run_units(act, unit)
            hi_of_gated(U - 1)

        @block.vector
        def _(dve):
            tt, stt, ts = nc.vector.tensor_tensor, nc.vector.scalar_tensor_tensor, nc.vector.tensor_scalar

            def lo_of_fill(b, u, f):
                bank, cols = dense[:, f, :], slice(f * HALF, (f + 1) * HALF)
                if b == "v":
                    return
                dve.wait_ge(hi_out[b], 2 * plan.projected(b, u) + f - 1)
                if b == "g":
                    stt(out=gate[:, cols], in0=gate[:, cols], scalar=1.0, in1=bank, op0=ALU.add,
                        op1=ALU.mult).then_inc(drained[b], 1)
                if b == "q":
                    for h in range(2):
                        last = stt(out=q_st[HD:P, h, cols], in0=bank[h * HD:(h + 1) * HD, :],
                                   scalar=SCALE / plan.kind(u).slope(u, h), in1=q_st[0:HD, h, cols], op0=ALU.mult, op1=ALU.subtract)
                    last.then_inc(drained[b], 1)
                if b == "k":
                    for h in range(2):
                        last = tt(k_l0[0:HD, h, cols], bank[h * HD:(h + 1) * HD, :], k_hh[0:HD, h, cols], ALU.subtract)
                    last.then_inc(drained[b], 1)

            def add_out(u, f):
                dve.wait_ge(filled["o"], FILLS["o"] * u + f + 1)
                if f == 0:
                    ge(dve, drained["o"], FILLS["o"] * u)
                    if plan.kind(u).name == "A":
                        dve.wait_ge(s_root, u + 1)
                        nc.vector.reciprocal(rms[:, 1, :], rms[:, 0, :]).then_inc(s_rroot, 1)
                        dve.wait_ge(s_rroot, u + 1)
                into = y[:, f // 2, (f % 2) * HALF:(f % 2 + 1) * HALF]
                if plan.kind(u).name == "A":
                    stt(out=into, in0=dense[:, 2, :], scalar=rms[:, 1, f // 2:f // 2 + 1], in1=into, op0=ALU.mult,
                        op1=ALU.add).then_inc(drained["o"], 1)
                else:
                    tt(into, dense[:, 2, :], into, ALU.add).then_inc(drained["o"], 1)

            def lowest(u, j):
                kind = plan.kind(u)
                h, t = kind.step(j)
                n = kind.tiles(t)[1]
                n1 = n * P if n <= 4 else {5: 256, 6: 384, 7: 384, 8: 512}[n]
                off = HALF - n1 if n > 4 else score_bank(kind, j) * HALF
                n *= P
                tile = bias_b if kind.name == "B" else bias
                slot, width = h if LOOP else 0, tile.shape[2]
                g = (j - 4) // 2 if kind.name == "A" else j - 4
                ge_apart(dve, s_passed, (s_scores, NS * u + j + 1),
                         (s_bias, (u + 1 if LOOP else kind.name == "B") if j == 0 else 0),
                         (s_turn, groups_before(u) + (g + 1 if j >= 4 else 0)))
                head = 2 * (u - kind.base) + h
                start = sinks[:, 1, head:head + 1] if kind.name == "B" else HUGE
                nc.vector.tensor_tensor_reduce(out=e_sb[:, e_of(j), 0:n], in0=scores[:, off:off + n],
                                               in1=tile[:, slot, width - n:width], scale=-kind.slope(u, h), scalar=start, op0=ALU.add,
                                               op1=ALU.min, accum_out=low[:, j:j + 1]).then_inc(s_low, 1)

            def normalise(u, j):
                kind = plan.kind(u)
                h, t = kind.step(j)
                n = kind.tiles(t)[1] * P
                e = e_sb[:, e_of(j), 0:n]
                ge(dve, s_exp, NS * u + j + 1)
                src = total
                if kind.name == "B":
                    dve.wait_ge(s_sink, NS * (u - kind.base) + j + 1)
                    tt(den[:, j:j + 1], total[:, j:j + 1], sink_e[:, j:j + 1], ALU.add).then_inc(s_den, 1)
                    dve.wait_ge(s_den, NS * (u - kind.base) + j + 1)
                    src = den
                nc.vector.reciprocal(rec[:, j:j + 1], src[:, j:j + 1]).then_inc(s_rec, 1)
                ge(dve, s_rec, NS * u + j + 1)
                if kind.name != "A":
                    ts(e, e, rec[:, j:j + 1], None, ALU.mult).then_inc(s_probs, 1)
                elif h == 1:
                    e0 = e_sb[:, e_of(j - 1), 0:n]
                    ts(e, e, rec[:, j:j + 1], neg_lam[:], ALU.mult, ALU.mult).then_inc(s_mid, 1)
                    dve.wait_ge(s_mid, groups_before(u) + j // 2 + 1)
                    stt(out=e0, in0=e0, scalar=rec[:, j - 1:j], in1=e, op0=ALU.mult, op1=ALU.add).then_inc(s_probs, 1)

            def lo_of_group(u, g):
                kind = plan.kind(u)
                h, t = kind.group(g)
                k0, n = kind.tiles(t)
                r = k0 - (t - t % 2) + 6 - R0
                q = slice((t % 2) * P, (t % 2 + 1) * P)
                ge(dve, s_phi, groups_before(u) + g + 1)
                tt(pT_lo[:, r:r + n, q], turned_group(kind, g, n), pT_hi[:, r:r + n, q],
                   ALU.subtract).then_inc(s_plo, 1)

            def out_sum(u, n):
                kind = plan.kind(u)
                if kind.name == "A":
                    return
                h, t = kind.group(2 * n)
                ge(dve, s_pvc, kind.pvs * (u - kind.base) + n + 1)
                o = o_sb[h * HD:(h + 1) * HD, t * P:(t + 2) * P]
                tt(o, pv_ps[0:HD, n % 2, :], o, ALU.add).then_inc(s_out, 1)

            def lo_of_v(u):
                ge(dve, s_vhi, nth("v", u) + 1)
                if plan.kind(u).name == "A":
                    tt(v_st[:, 1, :, :], turned[:].rearrange("p (s f) -> p s f", s=ST), v_st[:, 0, :, :],
                       ALU.subtract).then_inc(s_vlo, 1)
                else:
                    tt(v_st[:, :, :, HD:P], turned[:].rearrange("p (s h f) -> p h s f", s=ST, h=2),
                       v_st[:, :, :, 0:HD], ALU.subtract).then_inc(s_vlo, 1)

            lo_of_v(0)

            def constants():
                dve.wait_ge(s_const, 96)
                for i in range(2):
                    nc.vector.tensor_tensor_reduce(out=lam_prod[:], in0=lam_in[:, 2 * i, :], in1=lam_in[:, 2 * i + 1, :],
                                                   scale=1.0, scalar=0.0, op0=ALU.mult, op1=ALU.add,
                                                   accum_out=lam_sum[:, i:i + 1]).then_inc(s_lam, 1)
                    dve.wait_ge(s_lam, i + 1)
                dve.wait_ge(s_lam, 3)
                stt(out=neg_lam[:], in0=lam_sum[:, 3:4], scalar=-LAM_INIT, in1=lam_sum[:, 2:3], op0=ALU.add,
                    op1=ALU.subtract).then_inc(s_lam, 1)
                ts(g_sub[:], g_sub[:], 0.5 * (1.0 - LAM_INIT), None, ALU.mult).then_inc(s_lam, 1)
                dve.wait_ge(s_lam, 5)
                ts(sinks[:, 1, :], sinks[:, 0, :], -1.0, None, ALU.mult).then_inc(s_negsink, 1)
                dve.wait_ge(s_negsink, 1)

            def gated(u):
                ge(dve, s_out, pvs_before(u + 1))
                ge(dve, drained["g"], 2 * (u + 1))
                if plan.kind(u).name == "A":
                    ge(dve, s_sq, u + 1)
                stt(out=o_sb[:], in0=o_sb[:], scalar=g_sub[:] if plan.kind(u).name == "A" else 0.5, in1=gate[:],
                    op0=ALU.mult, op1=ALU.mult).then_inc(s_y, 1)

            def gated_lo(u):
                ge(dve, s_yhi, u + 1)
                tt(yT_lo[:], o_sb[:], yT_hi[:], ALU.subtract).then_inc(s_ylo, 1)

            def unit(u, first, last):
                for s in range(NS + TAIL):
                    g = transposed_after(u, s - 1) if s >= 1 else None
                    if g is not None:
                        lo_of_group(u, g)
                    if 1 <= s <= NS:
                        lowest(u, s - 1)
                    if 0 <= s - 2 < NS:
                        normalise(u, s - 2)
                    if s == 1 and AB and first:
                        constants()
                    if s == 1 and not first and (LOOP or plan.per_unit(u - 1)):
                        lo_of_v(u)
                    if s == GATE_STEP and not first:
                        gated(u - 1)
                    if s == GATE_STEP + 1 and not first:
                        gated_lo(u - 1)
                    fills = out_fills(plan, first, s)
                    if len(fills) > 1:
                        add_out(u - 1, fills[0])
                    for b, v, f in done_fills(plan, u, first, last, s - 1) if s else ():
                        if b == "g":
                            lo_of_fill(b, v, f)
                    for b, v, f in done_fills(plan, u, first, last, s):
                        if b != "g":
                            lo_of_fill(b, v, f)
                    if len(fills) > 0:
                        add_out(u - 1, fills[-1])
                    if pv_in(u, s) is not None:
                        out_sum(u, pv_in(u, s))
            run_units(dve, unit)
            gated(U - 1)
            gated_lo(U - 1)


def build(nc, x, pre_norm_g, post_norm_g, w_in_ab, w_out_ab, diff_lambda_q1, diff_lambda_k1, diff_lambda_q2,
          diff_lambda_k2, diff_subln_g, swa_sinks, w_in_c, w_out_c, rel_bias, out):
    rel_rows = nc.dram_tensor("rel_rows_dram", [C_HEADS, REL_ROW], F32, kind="Internal")
    rel_tiles = nc.dram_tensor("rel_tiles_dram", [P, C_HEADS, C_BAND_COLS], F32, kind="Internal")
    x1 = nc.dram_tensor("x1_dram", [SEQ, D], F32, kind="Internal")
    with ExitStack() as ctx:
        env = {
            "phase_semaphores": [],
            "rel_stored": ctx.enter_context(nc.semaphore("rel_stored")),
        }
        for name, shape, dt in (("ident", [P, P], F32),
                                ("hT_hi", [P, DT, SEQ], F32R), ("hT_lo", [P, DT, SEQ], F32R),
                                ("y", [P, ST, D], F32),
                                ("w_f32", [P, 2, D], F32), ("w_hi", [P, 3, D], F32R), ("w_lo", [P, 3, D], F32R),
                                ("q_st", [P, 2, SEQ], F32R),
                                ("k_hh", [P, 2, SEQ], F32R), ("k_l0", [P, 2, SEQ], F32R),
                                ("vT", [P, SEQ], F32), ("bias", [P, 2 * C_BAND_COLS], F32),
                                ("yT_hi", [P, SEQ], F32R), ("yT_lo", [P, SEQ], F32R)):
            env[name] = ctx.enter_context(nc.sbuf_tensor(name, shape, dt))
        boundary_phase(nc, 0, env, x[0], None, None, pre_norm_g[0], PLAN_AB, w_in_ab[0],
                       dict(table=rel_bias[0], rows=rel_rows, tiles=rel_tiles, stored=env["rel_stored"]))
        mixer_phase(nc, PLAN_AB, env, w_in_ab[0], w_out_ab[0],
                    dict(q1=diff_lambda_q1[0], k1=diff_lambda_k1[0], q2=diff_lambda_q2[0], k2=diff_lambda_k2[0],
                         g=diff_subln_g[0], sinks=swa_sinks[0]))
        retire(nc, env)
        boundary_phase(nc, 1, env, x[0], x1.ap(), post_norm_g[0], pre_norm_g[1], PLAN_C, w_in_c[0])
        mixer_phase(nc, PLAN_C, env, w_in_c[0], w_out_c[0], {}, rel_tiles)
        boundary_phase(nc, 2, env, x1.ap(), out[0], post_norm_g[1], None)


INPUTS = ["x", "pre_norm_g", "post_norm_g", "w_in_ab", "w_out_ab", "diff_lambda_q1", "diff_lambda_k1", "diff_lambda_q2",
          "diff_lambda_k2", "diff_subln_g", "swa_sinks", "w_in_c", "w_out_c", "rel_bias"]


def kernel(**inputs):
    import concourse.bacc as bacc
    import numpy as np
    from concourse.bass_utils import run_bass_kernel_spmd

    nc = bacc.Bacc("TRN2", target_bir_lowering=False, num_devices=1, dynamic_dma_scratch_size=1024)
    arrays, aps = {}, {}
    for name in INPUTS:
        a = np.ascontiguousarray(inputs[name])
        arrays[f"in_{name}"] = a
        aps[name] = nc.dram_tensor(f"in_{name}", a.shape, mybir.dt.from_np(a.dtype), kind="ExternalInput").ap()
    out = nc.dram_tensor("out_x", (1, SEQ, D), F32, kind="ExternalOutput").ap()
    build(nc, out=out, **aps)
    r = run_bass_kernel_spmd(nc, [arrays], core_ids=[0])
    return r.results[0]["out_x"]
```
